# Optimizing a Trainium2 kernel written in Bass

```python
import jax, jax.numpy as jnp
from jax import lax
import numpy as np

D_MODEL = 1024
BATCH = 1
SEQ = 512
DEPTH = 1
DEC_BATCH = 1
DEC_SEQ = 512
PAST_LEN = 128

GRID_W = 64
N_MIXERS = 3
EPS = 1e-6

NA_HEADS = 16
NA_HEAD_DIM = D_MODEL // NA_HEADS
NA_MAX_KH = 8
NA_KW = 16

POOL_WINDOWS = (2, 4, 8, 16)
POOL_GROUPS = 4
POOL_GROUP_DIM = D_MODEL // POOL_GROUPS

GLA_HEADS = 4
GLA_DK = D_MODEL // 2
GLA_DV = D_MODEL
GLA_HEAD_K = GLA_DK // GLA_HEADS
GLA_HEAD_V = GLA_DV // GLA_HEADS
GLA_GATE_RANK = 16
GLA_GATE_TAU = 16.0
GLA_CHUNK = 64
GLA_IN_WIDTH = 2 * GLA_DK + 2 * GLA_DV + 2 * GLA_GATE_RANK

N_EXPERTS = 16
EC_CAPACITY = 2
D_EXPERT = 2048

kernel_name = 'hybrid_bidir_encoder_na_pool_gla_ec'

def _mixer_counts():
    n_a = len(range(0, DEPTH, N_MIXERS))
    n_b = len(range(1, DEPTH, N_MIXERS))
    n_c = len(range(2, DEPTH, N_MIXERS))
    return n_a, n_b, n_c

def rmsnorm(x, g):
    xf = x.astype(jnp.float32)
    ms = jnp.mean(xf * xf, axis=-1, keepdims=True)
    return (xf * lax.rsqrt(ms + EPS) * g.astype(jnp.float32)).astype(x.dtype)

def neighbourhood_attention(h, w_qkv, rpb, w_o):
    B, T, _ = h.shape
    rows = T // GRID_W
    kh = min(NA_MAX_KH, rows)
    qkv = jnp.einsum('btd,de->bte', h, w_qkv)
    q, k, v = jnp.split(qkv, 3, axis=-1)
    grid = (B, rows, GRID_W, NA_HEADS, NA_HEAD_DIM)
    q = q.reshape(grid) * (NA_HEAD_DIM ** -0.5)
    k = k.reshape(grid)
    v = v.reshape(grid)
    cols = jnp.arange(GRID_W)
    col_start = jnp.clip(cols - NA_KW // 2, 0, GRID_W - NA_KW)
    col_idx = col_start[:, None] + jnp.arange(NA_KW)[None, :]
    dc = col_idx - cols[:, None] + (NA_KW - 1)

    def one_row(args):
        r, q_r = args
        r0 = jnp.clip(r - kh // 2, 0, rows - kh)
        k_rows = lax.dynamic_slice_in_dim(k, r0, kh, axis=1)
        v_rows = lax.dynamic_slice_in_dim(v, r0, kh, axis=1)
        k_win = k_rows[:, :, col_idx]
        v_win = v_rows[:, :, col_idx]
        dr = r0 + jnp.arange(kh) - r + (NA_MAX_KH - 1)
        bias = rpb[:, dr[:, None, None], dc[None, :, :]]
        bias = jnp.transpose(bias, (0, 2, 1, 3)).astype(jnp.float32)
        s = jnp.einsum('bchd,bicjhd->bhcij', q_r, k_win).astype(jnp.float32) + bias[None]
        p = jax.nn.softmax(s.reshape(B, NA_HEADS, GRID_W, kh * NA_KW), axis=-1)
        p = p.reshape(B, NA_HEADS, GRID_W, kh, NA_KW).astype(v.dtype)
        return jnp.einsum('bhcij,bicjhd->bchd', p, v_win)

    out = lax.map(one_row, (jnp.arange(rows), jnp.moveaxis(q, 1, 0)))
    out = jnp.moveaxis(out, 0, 1).reshape(B, T, D_MODEL)
    return jnp.einsum('btd,de->bte', out, w_o)

def multiscale_pool(h, pool_w, pool_scale):
    B, T, _ = h.shape
    hf = h.astype(jnp.float32)
    csum = jnp.concatenate([jnp.zeros((B, 1, D_MODEL), jnp.float32), jnp.cumsum(hf, axis=1)], axis=1)
    t = jnp.arange(T)
    groups = []
    for g, w in enumerate(POOL_WINDOWS):
        lo = jnp.clip(t - w // 2, 0, T)
        hi = jnp.clip(t + w - w // 2, 0, T)
        cs_g = csum[..., g * POOL_GROUP_DIM:(g + 1) * POOL_GROUP_DIM]
        cnt = (hi - lo).astype(jnp.float32)[None, :, None]
        mean = (cs_g[:, hi] - cs_g[:, lo]) / cnt
        groups.append(mean - hf[..., g * POOL_GROUP_DIM:(g + 1) * POOL_GROUP_DIM])
    pooled = jnp.stack(groups, axis=2)
    mixed = jnp.einsum('btgi,gio->btgo', pooled, pool_w.astype(jnp.float32)).reshape(B, T, D_MODEL)
    return (mixed * pool_scale.astype(jnp.float32)).astype(h.dtype)

def gla_chunked(q, k, v, log_a, include_diag):
    B, T, H, dk = q.shape
    dv = v.shape[-1]
    n = T // GLA_CHUNK
    q = q.reshape(B, n, GLA_CHUNK, H, dk)
    k = k.reshape(B, n, GLA_CHUNK, H, dk)
    v = v.reshape(B, n, GLA_CHUNK, H, dv)
    b = jnp.cumsum(log_a.reshape(B, n, GLA_CHUNK, H, dk), axis=2)
    b_last = b[:, :, -1:]
    q_dec = q * jnp.exp(b)
    k_inv = k * jnp.exp(-b)
    k_to_end = k * jnp.exp(b_last - b)
    scores = jnp.einsum('bnihk,bnjhk->bnhij', q_dec, k_inv)
    mask = jnp.tril(jnp.ones((GLA_CHUNK, GLA_CHUNK), dtype=bool), k=0 if include_diag else -1)
    o_intra = jnp.einsum('bnhij,bnjhv->bnihv', jnp.where(mask, scores, 0.0), v)
    kv = jnp.einsum('bnjhk,bnjhv->bnhkv', k_to_end, v)
    decay = jnp.exp(b_last[:, :, 0])

    def step(S, inp):
        kv_c, dec_c = inp
        return S * dec_c[..., None] + kv_c, S

    S0 = jnp.zeros((B, H, dk, dv), jnp.float32)
    _, S_prev = lax.scan(step, S0, (jnp.moveaxis(kv, 1, 0), jnp.moveaxis(decay, 1, 0)))
    S_prev = jnp.moveaxis(S_prev, 0, 1)
    o_inter = jnp.einsum('bnihk,bnhkv->bnihv', q_dec, S_prev)
    return (o_intra + o_inter).reshape(B, T, H, dv)

def gla_mixer(h, w_in, w_gate_f, b_gate_f, w_gate_b, b_gate_b, norm_g, w_o):
    B, T, _ = h.shape
    proj = jnp.einsum('btd,de->bte', h, w_in).astype(jnp.float32)
    s1, s2, s3, s4 = GLA_DK, 2 * GLA_DK, 2 * GLA_DK + GLA_DV, 2 * GLA_DK + 2 * GLA_DV
    q = proj[..., :s1].reshape(B, T, GLA_HEADS, GLA_HEAD_K) * (GLA_HEAD_K ** -0.5)
    k = proj[..., s1:s2].reshape(B, T, GLA_HEADS, GLA_HEAD_K)
    v = proj[..., s2:s3].reshape(B, T, GLA_HEADS, GLA_HEAD_V)
    r = proj[..., s3:s4]
    lr_f = proj[..., s4:s4 + GLA_GATE_RANK]
    lr_b = proj[..., s4 + GLA_GATE_RANK:]
    log_a_f = jax.nn.log_sigmoid(lr_f @ w_gate_f.astype(jnp.float32) + b_gate_f.astype(jnp.float32)) / GLA_GATE_TAU
    log_a_b = jax.nn.log_sigmoid(lr_b @ w_gate_b.astype(jnp.float32) + b_gate_b.astype(jnp.float32)) / GLA_GATE_TAU
    log_a_f = log_a_f.reshape(B, T, GLA_HEADS, GLA_HEAD_K)
    log_a_b = log_a_b.reshape(B, T, GLA_HEADS, GLA_HEAD_K)
    o_f = gla_chunked(q, k, v, log_a_f, True)
    fl = lambda a: jnp.flip(a, axis=1)
    o_b = fl(gla_chunked(fl(q), fl(k), fl(v), fl(log_a_b), False))
    o = o_f + o_b
    o = o * lax.rsqrt(jnp.mean(o * o, axis=-1, keepdims=True) + EPS)
    o = o * norm_g.astype(jnp.float32).reshape(GLA_HEADS, GLA_HEAD_V)
    o = o.reshape(B, T, GLA_DV) * jax.nn.silu(r)
    return jnp.einsum('btv,vd->btd', o.astype(h.dtype), w_o)

def expert_choice_ffn(h, router_w, w_gate, w_up, w_down):
    B, T, D = h.shape
    n = B * T
    cap = EC_CAPACITY * n // N_EXPERTS
    xf = h.reshape(n, D)
    aff = jax.nn.softmax(jnp.einsum('nd,de->ne', xf, router_w).astype(jnp.float32), axis=-1)
    gate, idx = lax.top_k(aff.T, cap)
    xs = xf[idx]
    hid = jax.nn.silu(jnp.einsum('ecd,edf->ecf', xs, w_gate)) * jnp.einsum('ecd,edf->ecf', xs, w_up)
    out = jnp.einsum('ecf,efd->ecd', hid, w_down) * gate[..., None].astype(xs.dtype)
    y = jnp.zeros_like(xf).at[idx.reshape(-1)].add(out.reshape(-1, D).astype(xf.dtype))
    return y.reshape(B, T, D)

def trunk(x, norm_mix_g, norm_ffn_g, final_norm_g, na_w_qkv, na_rpb, na_w_o, pool_w, pool_scale,
          gla_w_in, gla_w_gate_f, gla_b_gate_f, gla_w_gate_b, gla_b_gate_b, gla_norm_g, gla_w_o,
          router_w, moe_w_gate, moe_w_up, moe_w_down):
    h = x
    ia, ib, ic = 0, 0, 0
    for i in range(DEPTH):
        u = rmsnorm(h, norm_mix_g[i])
        kind = i % N_MIXERS
        if kind == 0:
            mix = neighbourhood_attention(u, na_w_qkv[ia], na_rpb[ia], na_w_o[ia])
            ia += 1
        elif kind == 1:
            mix = multiscale_pool(u, pool_w[ib], pool_scale[ib])
            ib += 1
        else:
            mix = gla_mixer(u, gla_w_in[ic], gla_w_gate_f[ic], gla_b_gate_f[ic], gla_w_gate_b[ic],
                            gla_b_gate_b[ic], gla_norm_g[ic], gla_w_o[ic])
            ic += 1
        h = h + mix.astype(h.dtype)
        u = rmsnorm(h, norm_ffn_g[i])
        h = h + expert_choice_ffn(u, router_w[i], moe_w_gate[i], moe_w_up[i], moe_w_down[i]).astype(h.dtype)
    return rmsnorm(h, final_norm_g)

def setup_inputs(seed: int = 0) -> dict:
    key = jax.random.key(seed)
    ks = jax.random.split(key, 24)
    n_a, n_b, n_c = _mixer_counts()
    nrm = jax.random.normal
    f32 = jnp.float32
    return {
        'x_prompt': nrm(ks[0], (BATCH, SEQ, D_MODEL), f32),
        'x_sample': nrm(ks[1], (DEC_BATCH, DEC_SEQ, D_MODEL), f32),
        'norm_mix_g': 1.0 + 0.02 * nrm(ks[2], (DEPTH, D_MODEL), f32),
        'norm_ffn_g': 1.0 + 0.02 * nrm(ks[3], (DEPTH, D_MODEL), f32),
        'final_norm_g': 1.0 + 0.02 * nrm(ks[4], (D_MODEL,), f32),
        'na_w_qkv': nrm(ks[5], (n_a, D_MODEL, 3 * D_MODEL), f32) * D_MODEL ** -0.5,
        'na_rpb': 0.02 * nrm(ks[6], (n_a, NA_HEADS, 2 * NA_MAX_KH - 1, 2 * NA_KW - 1), f32),
        'na_w_o': nrm(ks[7], (n_a, D_MODEL, D_MODEL), f32) * D_MODEL ** -0.5,
        'pool_w': nrm(ks[8], (n_b, POOL_GROUPS, POOL_GROUP_DIM, POOL_GROUP_DIM), f32) * POOL_GROUP_DIM ** -0.5,
        'pool_scale': 1.0 + 0.02 * nrm(ks[9], (n_b, D_MODEL), f32),
        'gla_w_in': nrm(ks[10], (n_c, D_MODEL, GLA_IN_WIDTH), f32) * D_MODEL ** -0.5,
        'gla_w_gate_f': nrm(ks[11], (n_c, GLA_GATE_RANK, GLA_DK), f32) * GLA_GATE_RANK ** -0.5,
        'gla_b_gate_f': 0.1 * nrm(ks[12], (n_c, GLA_DK), f32),
        'gla_w_gate_b': nrm(ks[13], (n_c, GLA_GATE_RANK, GLA_DK), f32) * GLA_GATE_RANK ** -0.5,
        'gla_b_gate_b': 0.1 * nrm(ks[14], (n_c, GLA_DK), f32),
        'gla_norm_g': 1.0 + 0.02 * nrm(ks[15], (n_c, GLA_DV), f32),
        'gla_w_o': nrm(ks[16], (n_c, GLA_DV, D_MODEL), f32) * GLA_DV ** -0.5,
        'router_w': nrm(ks[17], (DEPTH, D_MODEL, N_EXPERTS), f32) * D_MODEL ** -0.5,
        'moe_w_gate': nrm(ks[18], (DEPTH, N_EXPERTS, D_MODEL, D_EXPERT), f32) * D_MODEL ** -0.5,
        'moe_w_up': nrm(ks[19], (DEPTH, N_EXPERTS, D_MODEL, D_EXPERT), f32) * D_MODEL ** -0.5,
        'moe_w_down': nrm(ks[20], (DEPTH, N_EXPERTS, D_EXPERT, D_MODEL), f32) * D_EXPERT ** -0.5,
    }

def reference(x_prompt, x_sample, norm_mix_g, norm_ffn_g, final_norm_g, na_w_qkv, na_rpb, na_w_o,
              pool_w, pool_scale, gla_w_in, gla_w_gate_f, gla_b_gate_f, gla_w_gate_b, gla_b_gate_b,
              gla_norm_g, gla_w_o, router_w, moe_w_gate, moe_w_up, moe_w_down):
    y_prompt = trunk(x_prompt, norm_mix_g, norm_ffn_g, final_norm_g, na_w_qkv, na_rpb, na_w_o, pool_w,
                     pool_scale, gla_w_in, gla_w_gate_f, gla_b_gate_f, gla_w_gate_b, gla_b_gate_b,
                     gla_norm_g, gla_w_o, router_w, moe_w_gate, moe_w_up, moe_w_down)
    y_sample = trunk(x_sample, norm_mix_g, norm_ffn_g, final_norm_g, na_w_qkv, na_rpb, na_w_o, pool_w,
                     pool_scale, gla_w_in, gla_w_gate_f, gla_b_gate_f, gla_w_gate_b, gla_b_gate_b,
                     gla_norm_g, gla_w_o, router_w, moe_w_gate, moe_w_up, moe_w_down)
    return (y_prompt, y_sample)


_drawn_inputs = setup_inputs


def setup_inputs(seed=0):
    import zlib

    import numpy as np

    out = dict(_drawn_inputs(seed))
    spreads = {}
    factors = {'norm_mix_g': 5.91, 'norm_ffn_g': 3.479, 'final_norm_g': 2.87, 'na_rpb': 7.863}
    for name, (base, spread) in spreads.items():
        noise = np.random.default_rng([zlib.crc32(name.encode()), seed]).standard_normal(out[name].shape)
        drawn = base * np.exp(spread * noise) if base else spread * noise
        out[name] = __import__('jax').numpy.asarray(drawn.astype(out[name].dtype))
    for name, factor in factors.items():
        out[name] = (out[name] * factor).astype(out[name].dtype)
    return out
```

```python
import numpy as np
import concourse.bass as bass
from concourse import mybir
from contextlib import ExitStack

F32 = mybir.dt.float32
F32R = mybir.dt.float32r
U32 = mybir.dt.uint32
ALU = mybir.AluOpType
ACT = mybir.ActivationFunctionType
AX = mybir.AxisListType

P = 128
D = 1024
T = 512
TRUNKS = 2
GRID_W = 64
ROWS = T // GRID_W
KW = 16
KH = 8
HEADS = 16
HD = D // HEADS
E = 16
CAP = 2 * T // E
F = 2048
EPS = 1e-6
MASKED = -1e30

KC = D // P
TILES = T // P
QCOLS = GRID_W // TILES
WIN = 2 * P
WIN_COL = [min(max(QCOLS * i - KW // 2, 0), GRID_W - WIN // ROWS) for i in range(TILES)]
KIND = [0, 1, 1, 2]
GROUP = 4
GROUPS = HEADS // GROUP
GC = GROUP * HD
SLOTS = 4
PAIR = 2048
HALF = F // 2
BANK = 512
FRONT_Q = TRUNKS * GROUPS
GU_PAIRS = 8
D_PAIRS = 4
HT_AFTER = 6


def encoder_kernel(nc, x, g_mix, g_ffn, g_fin, w_qkv, bias, w_o, router_w, w_gate, w_up, w_down, identity, y):
    h_dram = nc.dram_tensor("h_rows", [TRUNKS * T, D], F32).ap()
    u_dram = nc.dram_tensor("u_rows", [TRUNKS * T, D], F32).ap()
    wqkv_v = w_qkv.rearrange("(k p) n -> p k n", p=P)
    wo_v = w_o.rearrange("(k p) n -> p k n", p=P)

    with ExitStack() as ctx:
        def sb(name, shape, dt=F32):
            return ctx.enter_context(nc.sbuf_tensor(name, shape, dt))

        def sem(name):
            return ctx.enter_context(nc.semaphore(name))

        raw = sb("raw", [P, SLOTS, PAIR])
        w_high = sb("w_high", [P, SLOTS, PAIR], F32R)
        w_rest = sb("w_rest", [P, SLOTS, PAIR], F32R)
        xh = sb("xh", [P, TILES, D])
        arena = sb("arena", [P, TILES, D])
        ut_high = sb("ut_high", [P, KC * T], F32R)
        ut_rest = sb("ut_rest", [P, KC * T], F32R)
        qz = sb("qz", [P, 2, 2, T])
        kt = sb("kt", [P, 2, T])
        v = sb("v", [P, TILES, GC])
        v_off = sb("v_off", [P, TILES - 1, GC])
        bias_sb = sb("bias_sb", [P, 2, 3, WIN])
        o = sb("o", [P, TILES, GC])
        ot_high = sb("ot_high", [P, 2, T], F32R)
        ot_rest = sb("ot_rest", [P, 2, T], F32R)
        grow = sb("grow", [P, D])
        ident = sb("ident", [P, P])
        rw = sb("rw", [P, KC, E])
        aff = sb("aff", [P, TILES, TRUNKS * E])
        lg = sb("lg", [P, TILES, E])
        ssq = sb("ssq", [P, 24])
        var = sb("var", [P, 24])
        sdev = sb("sdev", [P, 24])
        rstd = sb("rstd", [P, 24])
        newt = sb("newt", [P, 3, 24])
        mx = sb("mx", [P, 2, TILES])
        nmx = sb("nmx", [P, 2, TILES])
        psum_row = sb("psum_row", [P, 2, TILES])
        rinv = sb("rinv", [P, 2, TILES])
        lstat = sb("lstat", [P, TRUNKS, 3, TILES])
        topv = sb("topv", [TRUNKS * E, CAP])
        topi = sb("topi", [TRUNKS * E, CAP], U32)
        topt = sb("topt", [TRUNKS * E, 3, CAP], U32)
        gv = sb("gv", [TRUNKS * E, 2, CAP])
        gi = sb("gi", [TRUNKS * E, 2, CAP])
        gate_w = sb("gate_w", [P, E])
        rows = sb("rows", [P, E], U32)

        scores = arena[:, 0:2, :].rearrange("p s (i k) -> p s i k", i=TILES)
        pt = arena[:, 2:4, :]
        affw = arena[0:TRUNKS * E, 0, 0:T]
        xg = xh[:, 0, :]
        silu = xh[:, 1, :]
        hid = xh[:, 2, :]
        ys = xh[:, 3, :]
        xt_high = ut_high[:, 0:D]
        xt_rest = ut_rest[:, 0:D]
        ht_high = ut_high[:, D:2 * D]
        ht_rest = ut_rest[:, D:2 * D]

        ps = ctx.enter_context(nc.psum_tensor("ps", [P, 8 * BANK], F32))

        def bank(b, n=1):
            return ps[:, b * BANK:(b + n) * BANK]

        const_in = sem("const_in")
        bias_in = [sem(f"bias_in{s}") for s in range(2)]
        x_in = sem("x_in")
        grow_in = sem("grow_in")
        raw_in = [sem(f"raw_in{j}") for j in range(SLOTS)]
        voff_in = sem("voff_in")
        h_out = sem("h_out")
        u_out = sem("u_out")
        gathered = sem("gathered")
        scattered = sem("scattered")
        ys_free = sem("ys_free")
        h_in = [sem(f"h_in{c}") for c in range(TRUNKS)]
        y_out = sem("y_out")
        high_done = sem("high_done")
        rest_done = sem("rest_done")
        pair_used = sem("pair_used")
        zeros_done = sem("zeros_done")
        ssq_done = sem("ssq_done")
        var_done = sem("var_done")
        sdev_done = sem("sdev_done")
        norm_step = sem("norm_step")
        xs_done = sem("xs_done")
        xt_front = sem("xt_front")
        uth_done = sem("uth_done")
        utr_done = sem("utr_done")
        q_done, k_done, v_done = sem("q_done"), sem("k_done"), sem("v_done")
        s_mm = sem("s_mm")
        max_done = sem("max_done")
        nmx_done = sem("nmx_done")
        exp_done = sem("exp_done")
        pt_mm = sem("pt_mm")
        pt_act, pt_dve = sem("pt_act"), sem("pt_dve")
        pv_mm = sem("pv_mm")
        rinv_done = sem("rinv_done")
        o_done = sem("o_done")
        ot_mm = sem("ot_mm")
        oth_done, otr_done = sem("oth_done"), sem("otr_done")
        wo_mm = sem("wo_mm")
        h_done = sem("h_done")
        rt_mm = sem("rt_mm")
        rt_copied = sem("rt_copied")
        rt_used = sem("rt_used")
        lg_step = sem("lg_step")
        lexp_done = sem("lexp_done")
        aff_done = sem("aff_done")
        afft_mm = sem("afft_mm")
        top_step = sem("top_step")
        top_done = sem("top_done")
        route_mm = sem("route_mm")
        route_done = sem("route_done")
        xt_mm, xth_done, xtr_done = sem("xt_mm"), sem("xth_done"), sem("xtr_done")
        silu_done, hid_done = sem("silu_done"), sem("hid_done")
        ht_mm, hth_done, htr_done = sem("ht_mm"), sem("hth_done"), sem("htr_done")
        ys_done = sem("ys_done")
        fin_done = sem("fin_done")

        block = ctx.enter_context(nc.Block())

        def body_q(e, i):
            return FRONT_Q + GU_PAIRS // SLOTS + (2 * (GU_PAIRS + D_PAIRS) // SLOTS) * e + i // SLOTS

        @block.sync
        def _(sp):
            sp.dma_start(ident[:, :], identity).then_inc(const_in, 16)
            sp.dma_start(rw[:, :, :], router_w.rearrange("(k p) e -> p k e", p=P)).then_inc(const_in, 16)

            def load(q, j, src, first=False):
                if not first:
                    sp.wait_ge(rest_done, SLOTS * (q - 1) + j + 1)
                sp.dma_start(raw[:, j, :].rearrange("p (k n) -> p k n", k=src.shape[1]), src).then_inc(raw_in[j], 16)

            def load_group(G, g, j, first=False):
                if j < 3:
                    load(G, j, wqkv_v[:, :, bass.ds(j * D + g * GC, GC)], first)
                else:
                    load(G, j, wo_v[:, bass.ds(2 * g, 2), :], first)

            def load_bias(G, g, hh, first=False):
                if not first:
                    sp.wait_ge(max_done, TILES * (GROUP * G + hh - 1))
                sp.dma_start(bias_sb[:, hh % 2, :, :].rearrange("p a k -> p (a k)"),
                             bias[bass.ds((g * GROUP + hh) * P, P), :]).then_inc(bias_in[hh % 2], 16)

            def load_gate_up(e, h, q_of, lo=0, hi=GU_PAIRS):
                for jj in range(lo, hi):
                    src = (w_gate, w_up)[jj % 2]
                    rows_ = src[bass.ds(e * D + (jj // 2) * 2 * P, 2 * P), h * HALF:(h + 1) * HALF]
                    load(q_of(jj), jj % SLOTS, rows_.rearrange("(k p) n -> p k n", p=P))

            def load_down(e, h, q_of):
                for jj in range(D_PAIRS):
                    rows_ = w_down[bass.ds(e * F + h * HALF + jj * 2 * P, 2 * P), :]
                    load(q_of(jj), jj % SLOTS, rows_.rearrange("(k p) n -> p k n", p=P))

            def group(G, g, load_next, first=False):
                load_bias(G, g, 0, first)
                load_bias(G, g, 1, first)
                load_next()
                load_bias(G, g, 2)
                load_bias(G, g, 3)

            def next_pairs(G, g):
                return lambda: [load_group(G, g, j) for j in range(SLOTS)]

            for j in range(SLOTS):
                load_group(0, 0, j, first=True)
            group(0, 0, next_pairs(1, 1), first=True)
            with sp.Fori(1, GROUPS - 1) as g:
                group(g, g, next_pairs(g + 1, g + 1))
            group(GROUPS - 1, GROUPS - 1, next_pairs(GROUPS, 0))
            with sp.Fori(0, GROUPS - 1) as g:
                group(g + GROUPS, g, next_pairs(g + GROUPS + 1, g + 1))
            first_q = lambda i: FRONT_Q + i // SLOTS
            group(2 * GROUPS - 1, GROUPS - 1, lambda: load_gate_up(0, 0, first_q, 0, SLOTS))
            load_gate_up(0, 0, first_q, SLOTS, GU_PAIRS)
            with sp.Fori(0, E - 1) as e:
                at = lambda s: lambda i: body_q(e, s + i)
                load_gate_up(e, 1, at(0))
                load_down(e, 0, at(GU_PAIRS))
                load_gate_up(e + 1, 0, at(GU_PAIRS + D_PAIRS))
                load_down(e, 1, at(2 * GU_PAIRS + D_PAIRS))
            at = lambda s: lambda i: body_q(E - 1, s + i)
            load_gate_up(E - 1, 1, at(0))
            load_down(E - 1, 0, at(GU_PAIRS))
            load_down(E - 1, 1, at(GU_PAIRS + D_PAIRS))

            sp.wait_ge(scattered, 16 * E)
            sp.dma_start(xh[:, :, :], h_dram[0:T, :].rearrange("(i p) d -> p i d", p=P)).then_inc(h_in[0], 16)
            sp.dma_start(arena[:, :, :], h_dram[T:2 * T, :].rearrange("(i p) d -> p i d", p=P)).then_inc(h_in[1], 16)
            for c, buf in enumerate((xh, arena)):
                for i in range(TILES):
                    sp.wait_ge(fin_done, c * TILES + i + 1)
                    sp.dma_start(y[c * T + i * P:c * T + (i + 1) * P, :], buf[:, i, :]).then_inc(y_out, 16)
            sp.wait_ge(y_out, 16 * TRUNKS * TILES)

        @block.gpsimd
        def _(pool):
            def load_grow(g):
                pool.dma_start(grow[:, :], g.broadcast_to([P, D])).then_inc(grow_in, 16)

            nc.gpsimd.memset(qz[HD:P, 0, :, :], 0.0).then_inc(zeros_done, 1)
            nc.gpsimd.memset(qz[0:HD, 1, :, :], 0.0).then_inc(zeros_done, 1)
            for b in range(TRUNKS):
                if b:
                    pool.wait_ge(xs_done, TILES * 2 * b)
                    pool.wait_ge(h_out, 16 * b)
                pool.dma_start(xh[:, :, :], x[b * T:(b + 1) * T, :].rearrange("(i p) d -> p i d", p=P)).then_inc(x_in, 16)
                load_grow(g_mix)
                pool.wait_ge(xs_done, TILES * (2 * b + 1))
                load_grow(g_ffn)
                pool.wait_ge(h_done, GROUPS * TILES * (b + 1) + TILES)
                pool.dma_start(h_dram[b * T:(b + 1) * T, :].rearrange("(i p) d -> p i d", p=P), xh[:, :, :]).then_inc(h_out, 16)
                pool.wait_ge(xs_done, TILES * 2 * (b + 1))
                pool.dma_start(u_dram[b * T:(b + 1) * T, :].rearrange("(i p) d -> p i d", p=P), arena[:, :, :]).then_inc(u_out, 16)
            load_grow(g_fin)

            def gather(e):
                pool.indirect_dma_start(xg, None, u_dram, bass.IndirectOffsetOnAxis(ap=rows[:, e:e + 1], axis=0)).then_inc(gathered, 16)

            pool.sem_inc(ys_free, 1)
            pool.wait_ge(u_out, 16 * TRUNKS)
            pool.wait_ge(h_out, 16 * TRUNKS)
            pool.wait_ge(route_done, 1)
            gather(0)
            for e in range(E):
                if e + 1 < E:
                    pool.wait_ge(xt_mm, e + 1)
                    gather(e + 1)
                if e:
                    pool.wait_ge(scattered, 16 * e)
                    pool.sem_inc(ys_free, 1)
                pool.wait_ge(ys_done, e + 2)
                pool.indirect_dma_start(h_dram, bass.IndirectOffsetOnAxis(ap=rows[:, e:e + 1], axis=0), ys, None,
                                        compute_op=ALU.add).then_inc(scattered, 16)
            pool.wait_ge(scattered, 16 * E)

        @block.scalar
        def _(act):
            def high(q, j, free=False):
                act.wait_ge(raw_in[j], 16 * (q + 1))
                if not free:
                    act.wait_ge(pair_used, SLOTS * (q - 1) + j + 1)
                nc.scalar.copy(w_high[:, j, :], raw[:, j, :]).then_inc(high_done, 1)

            def squares(c, src, junk):
                for i in range(TILES):
                    nc.scalar.activation(junk(i), src[:, i, :], ACT.Square, accum_out=ssq[:, TILES * c + i:TILES * c + i + 1]).then_inc(ssq_done, 1)
                act.wait_ge(var_done, c + 1)
                nc.scalar.activation(sdev[:, TILES * c:TILES * (c + 1)], var[:, TILES * c:TILES * (c + 1)], ACT.Sqrt).then_inc(sdev_done, 1)

            def exponentials(A, s):
                act.wait_ge(nmx_done, A + 1)
                for i in range(TILES):
                    nc.scalar.activation(scores[:, s, i, :], scores[:, s, i, :], ACT.Exp, bias=nmx[:, s, i:i + 1],
                                         accum_out=psum_row[:, s, i:i + 1]).then_inc(exp_done, 1)

            def copy_pt(A, s):
                act.wait_ge(pt_mm, A + 1)
                nc.scalar.copy(pt[:, s, 512:1024], bank(3)).then_inc(pt_act, 1)

            def group(G):
                act.wait_ge(pair_used, SLOTS * G + 1)
                for m in range(2):
                    for half in range(2):
                        part = slice(HD * half, HD * (half + 1))
                        nc.scalar.mul(qz[part, half, m, :], bank(m)[part, :], HD ** -0.5).then_inc(q_done, 1)
                act.wait_ge(pair_used, SLOTS * G + 3)
                nc.scalar.copy(v[:, :, :].rearrange("p i n -> p (i n)"), bank(4, 2)).then_inc(v_done, 1)
                act.wait_ge(v_done, G + 1)
                act.dma_start(v_off[0:HD, :, :], v[HD:P, 0:TILES - 1, :]).then_inc(voff_in, 16)
                act.dma_start(v_off[HD:P, :, :], v[0:HD, 1:TILES, :]).then_inc(voff_in, 16)
                high(G, 3, free=True)
                exponentials(GROUP * G, 0)
                high(G + 1, 0)
                exponentials(GROUP * G + 1, 1)
                copy_pt(GROUP * G, 0)
                high(G + 1, 1)
                exponentials(GROUP * G + 2, 0)
                copy_pt(GROUP * G + 1, 1)
                high(G + 1, 2)
                exponentials(GROUP * G + 3, 1)
                copy_pt(GROUP * G + 2, 0)
                copy_pt(GROUP * G + 3, 1)
                for f in range(2):
                    act.wait_ge(ot_mm, 2 * G + f + 1)
                    nc.scalar.copy(ot_high[:, f, :], bank(f)).then_inc(oth_done, 1)

            act.sem_inc(ys_done, 1)
            for b in range(TRUNKS):
                act.wait_ge(x_in, 16 * (b + 1))
                if b:
                    act.wait_ge(u_out, 16 * b)
                squares(2 * b, xh, lambda i: arena[:, i, :])
                for kc in range(KC):
                    act.wait_ge(xt_front, KC * b + kc + 1)
                    nc.scalar.copy(ut_high[:, kc * T:(kc + 1) * T], bank(kc % 2)).then_inc(uth_done, 1)
                if b == 0:
                    for j in range(3):
                        high(0, j, free=True)
                with act.Fori(0, GROUPS) as g:
                    group(g + GROUPS * b)
                act.wait_ge(h_done, GROUPS * TILES * (b + 1) + TILES)
                squares(2 * b + 1, xh, lambda i: arena[:, i, :])
                for kc in range(KC):
                    act.wait_ge(rt_mm, KC * b + kc + 1)
                    if kc >= 2:
                        act.wait_ge(rt_used, KC * b + kc - 1)
                    nc.scalar.copy(kt[:, kc % 2, :], bank(kc % 2)).then_inc(rt_copied, 1)
                act.wait_ge(lg_step, 2 * (b + 1))
                nc.scalar.activation(lg[:, :, :], lg[:, :, :], ACT.Exp).then_inc(lexp_done, 1)

            def step_silu(s, used_by_gate_up):
                act.wait_ge(pair_used, used_by_gate_up)
                nc.scalar.activation(silu, bank(0, 2), ACT.Silu).then_inc(silu_done, 1)

            def rows_high(e):
                act.wait_ge(xt_mm, e + 1)
                nc.scalar.copy(xt_high, bank(6, 2)).then_inc(xth_done, 1)

            def hidden_high(s):
                act.wait_ge(ht_mm, s + 1)
                nc.scalar.copy(ht_high, bank(6, 2)).then_inc(hth_done, 1)

            def result(e, used_by_down):
                act.wait_ge(pair_used, used_by_down)
                act.wait_ge(ys_free, e + 1)
                nc.scalar.activation(ys, bank(4, 2), ACT.Copy, scale=gate_w[:, bass.ds(e, 1)]).then_inc(ys_done, 1)

            def highs(q_of, lo, hi):
                for i in range(lo, hi):
                    high(q_of(i), i % SLOTS)

            first_q = lambda i: FRONT_Q + i // SLOTS
            high(first_q(3), 3)
            rows_high(0)
            highs(first_q, 4, GU_PAIRS)
            step_silu(0, SLOTS * FRONT_Q + GU_PAIRS)
            last = lambda e: (lambda i: body_q(e, i))
            highs(last(0), 0, HT_AFTER)
            hidden_high(0)
            with act.Fori(0, E - 1) as e:
                highs(last(e), HT_AFTER, 12)
                step_silu(2 * e + 1, SLOTS * body_q(e, 0) + 8)
                rows_high(e + 1)
                highs(last(e), 12, 12 + HT_AFTER)
                hidden_high(2 * e + 1)
                highs(last(e), 12 + HT_AFTER, 24)
                step_silu(2 * e + 2, SLOTS * body_q(e, 0) + 20)
                highs(last(e + 1), 0, HT_AFTER)
                hidden_high(2 * e + 2)
                result(e, SLOTS * body_q(e, 0) + 24)
            highs(last(E - 1), HT_AFTER, 12)
            step_silu(2 * E - 1, SLOTS * body_q(E - 1, 0) + 8)
            highs(last(E - 1), 12, 16)
            hidden_high(2 * E - 1)
            result(E - 1, SLOTS * body_q(E - 1, 0) + 16)

            for c, buf in enumerate((xh, arena)):
                act.wait_ge(h_in[c], 16)
                squares(4 + c, buf, lambda i: raw[:, 2 * c + i // 2, (i % 2) * D:(i % 2 + 1) * D])

        @block.vector
        def _(dve):
            def rest(q, j):
                dve.wait_ge(high_done, SLOTS * q + j + 1)
                nc.vector.tensor_tensor(w_rest[:, j, :], raw[:, j, :], w_high[:, j, :].bitcast(F32), ALU.subtract).then_inc(rest_done, 1)

            def one_over_rms(c):
                cols = slice(TILES * c, TILES * (c + 1))
                dve.wait_ge(ssq_done, TILES * (c + 1))
                nc.vector.tensor_scalar(var[:, cols], ssq[:, cols], 1.0 / D, EPS, ALU.mult, ALU.add).then_inc(var_done, 1)
                dve.wait_ge(sdev_done, c + 1)
                n = 5 * c

                nc.vector.reciprocal(newt[:, 0, cols], sdev[:, cols]).then_inc(norm_step, 1)
                dve.wait_ge(norm_step, n + 1)
                nc.vector.tensor_tensor(newt[:, 1, cols], newt[:, 0, cols], newt[:, 0, cols], ALU.mult).then_inc(norm_step, 1)
                dve.wait_ge(norm_step, n + 2)
                nc.vector.tensor_tensor(newt[:, 2, cols], newt[:, 1, cols], var[:, cols], ALU.mult).then_inc(norm_step, 1)
                dve.wait_ge(norm_step, n + 3)
                nc.vector.tensor_scalar(newt[:, 1, cols], newt[:, 2, cols], -0.5, 1.5, ALU.mult, ALU.add).then_inc(norm_step, 1)
                dve.wait_ge(norm_step, n + 4)
                nc.vector.tensor_tensor(rstd[:, cols], newt[:, 0, cols], newt[:, 1, cols], ALU.mult).then_inc(norm_step, 1)
                dve.wait_ge(norm_step, n + 5)

            def normalise(c, dst, src, i, done):
                nc.vector.scalar_tensor_tensor(out=dst[:, i, :], in0=src[:, i, :], scalar=rstd[:, TILES * c + i:TILES * c + i + 1],
                                               in1=grow[:, :], op0=ALU.mult, op1=ALU.mult).then_inc(done, 1)

            def biased(A, G, s, hh):
                dve.wait_ge(s_mm, A + 1)
                dve.wait_ge(bias_in[hh % 2], 16 * (2 * G + hh // 2 + 1))
                nc.vector.memset(nmx[:, s, :], 0.0)
                base = (6, 0)[s]
                for i in range(TILES):
                    nc.vector.tensor_tensor_reduce(out=scores[:, s, i, :], in0=ps[:, base * BANK + i * WIN:base * BANK + (i + 1) * WIN],
                                                   in1=bias_sb[:, hh % 2, KIND[i], :], scale=1.0, scalar=-3e38, op0=ALU.add,
                                                   op1=ALU.max, accum_out=mx[:, s, i:i + 1]).then_inc(max_done, 1)
                dve.wait_ge(max_done, TILES * (A + 1))
                nc.vector.tensor_scalar(nmx[:, s, :], mx[:, s, :], -1.0, None, ALU.mult).then_inc(nmx_done, 1)

            def copy_pt(A, s):
                dve.wait_ge(pt_mm, A + 1)
                nc.vector.tensor_copy(pt[:, s, 0:512], bank(2)).then_inc(pt_dve, 1)

            def output(A, s, hh):
                nc.vector.reciprocal(rinv[:, s, :], psum_row[:, s, :]).then_inc(rinv_done, 1)
                dve.wait_ge(rinv_done, A + 1)
                dve.wait_ge(pv_mm, A + 1)
                nc.vector.tensor_tensor(o[:, :, hh * HD:(hh + 1) * HD],
                                        bank(4 + s)[:, 0:TILES * HD].rearrange("p (i n) -> p i n", i=TILES),
                                        rinv[:, s, :].rearrange("p (i a) -> p i a", a=1).broadcast_to([P, TILES, HD]), ALU.mult).then_inc(o_done, 1)

            def group(G):
                A = GROUP * G
                dve.wait_ge(pair_used, SLOTS * G + 2)
                nc.vector.tensor_copy(kt[:, :, :].rearrange("p m t -> p (m t)"), bank(2, 2)).then_inc(k_done, 1)
                rest(G, 3)
                biased(A, G, 0, 0)
                rest(G + 1, 0)
                biased(A + 1, G, 1, 1)
                copy_pt(A, 0)
                output(A, 0, 0)
                rest(G + 1, 1)
                biased(A + 2, G, 0, 2)
                copy_pt(A + 1, 1)
                output(A + 1, 1, 1)
                rest(G + 1, 2)
                biased(A + 3, G, 1, 3)
                copy_pt(A + 2, 0)
                output(A + 2, 0, 2)
                copy_pt(A + 3, 1)
                output(A + 3, 1, 3)
                for f in range(2):
                    dve.wait_ge(oth_done, 2 * G + f + 1)
                    nc.vector.tensor_tensor(ot_rest[:, f, :], bank(f), ot_high[:, f, :].bitcast(F32), ALU.subtract).then_inc(otr_done, 1)
                for i in range(TILES):
                    if i + 1 < TILES:
                        dve.wait_ge(wo_mm, (TILES - 1) * G + i + 1)
                    else:
                        dve.wait_ge(pair_used, SLOTS * (G + 1))
                    nc.vector.tensor_tensor(xh[:, i, :], bank(4 + 2 * (i % 2), 2), xh[:, i, :], ALU.add).then_inc(h_done, 1)

            dve.sem_inc(h_done, TILES)
            for b in range(TRUNKS):
                one_over_rms(2 * b)
                dve.wait_ge(grow_in, 16 * (2 * b + 1))
                for i in range(TILES):
                    normalise(2 * b, arena, xh, i, xs_done)
                for kc in range(KC):
                    dve.wait_ge(uth_done, KC * b + kc + 1)
                    nc.vector.tensor_tensor(ut_rest[:, kc * T:(kc + 1) * T], bank(kc % 2),
                                            ut_high[:, kc * T:(kc + 1) * T].bitcast(F32), ALU.subtract).then_inc(utr_done, 1)
                if b == 0:
                    for j in range(3):
                        rest(0, j)
                with dve.Fori(0, GROUPS) as g:
                    group(g + GROUPS * b)

                one_over_rms(2 * b + 1)
                dve.wait_ge(grow_in, 16 * (2 * b + 2))
                for i in range(TILES):
                    normalise(2 * b + 1, arena, xh, i, xs_done)
                dve.wait_ge(rt_used, KC * (b + 1))
                logits = bank(4, 4).rearrange("p (i n) -> p i n", i=TILES)[:, :, 0:E]
                spread = lambda a: a.rearrange("p (i a) -> p i a", a=1).broadcast_to([P, TILES, E])
                nc.vector.tensor_reduce(lstat[:, b, 0, :], logits, AX.X, ALU.max).then_inc(lg_step, 1)
                dve.wait_ge(lg_step, 2 * b + 1)
                nc.vector.tensor_tensor(lg[:, :, :], logits, spread(lstat[:, b, 0, :]), ALU.subtract).then_inc(lg_step, 1)
                dve.wait_ge(lexp_done, b + 1)
                nc.vector.tensor_reduce(lstat[:, b, 1, :], lg[:, :, :], AX.X, ALU.add).then_inc(aff_done, 1)
                dve.wait_ge(aff_done, 3 * b + 1)
                nc.vector.reciprocal(lstat[:, b, 2, :], lstat[:, b, 1, :]).then_inc(aff_done, 1)
                dve.wait_ge(aff_done, 3 * b + 2)
                nc.vector.tensor_tensor(aff[:, :, b * E:(b + 1) * E], lg[:, :, :], spread(lstat[:, b, 2, :]), ALU.mult).then_inc(aff_done, 1)
                if b == 0:
                    dve.wait_ge(u_out, 16)
                    dve.wait_ge(aff_done, 3)

            count = 0

            def link(instruction):
                nonlocal count
                count += 1
                instruction.then_inc(top_step, 1)
                dve.wait_ge(top_step, count)

            dve.wait_ge(u_out, 32)
            dve.wait_ge(afft_mm, 1)
            link(nc.vector.tensor_copy(affw.rearrange("e (r i c) -> e r i c", r=ROWS, i=TILES),
                                       bank(0)[0:TRUNKS * E, :].rearrange("e (i c r) -> e r i c", i=TILES, r=ROWS)))
            for k in range(CAP // 8):
                best = topv[:, 8 * k:8 * k + 8]
                link(nc.vector.max(best, affw))
                link(nc.vector.max_index(topi[:, 8 * k:8 * k + 8], best, affw))
                if k + 1 < CAP // 8:
                    link(nc.vector.match_replace(affw, best, affw, -1.0))
            link(nc.vector.tensor_scalar(topt[:, 0, :], topi[:, :], GRID_W - 1, ROWS.bit_length() - 1, ALU.bitwise_and, ALU.logical_shift_left))
            link(nc.vector.tensor_scalar(topt[:, 1, :], topi[:, :], GRID_W.bit_length() - 1, None, ALU.logical_shift_right))
            link(nc.vector.tensor_tensor(topt[:, 2, :], topt[:, 0, :], topt[:, 1, :], ALU.bitwise_or))
            for k in range(2):
                nc.vector.tensor_copy(gv[:, k, :], topv[:, :]).then_inc(top_done, 1)
                nc.vector.tensor_copy(gi[:, k, :], topt[:, 2, :]).then_inc(top_done, 1)
            dve.wait_ge(route_mm, 1)
            link(nc.vector.tensor_copy(gate_w[0:CAP, :], bank(1)[0:CAP, 0:E]))
            link(nc.vector.tensor_copy(gate_w[CAP:P, :], bank(1)[CAP:P, E:2 * E]))
            link(nc.vector.tensor_copy(rows[0:CAP, :], bank(1)[0:CAP, 2 * E:3 * E]))
            nc.vector.tensor_scalar(rows[CAP:P, :], bank(1)[CAP:P, 3 * E:4 * E], float(T), None, ALU.add).then_inc(route_done, 1)

            def step_hidden(s):
                dve.wait_ge(silu_done, s + 1)
                nc.vector.tensor_tensor(hid, bank(2, 2), silu, ALU.mult).then_inc(hid_done, 1)

            def rows_rest(e):
                dve.wait_ge(xth_done, e + 1)
                nc.vector.tensor_tensor(xt_rest, bank(6, 2), xt_high.bitcast(F32), ALU.subtract).then_inc(xtr_done, 1)

            def hidden_rest(s):
                dve.wait_ge(hth_done, s + 1)
                nc.vector.tensor_tensor(ht_rest, bank(6, 2), ht_high.bitcast(F32), ALU.subtract).then_inc(htr_done, 1)

            def rests(q_of, lo, hi):
                for i in range(lo, hi):
                    rest(q_of(i), i % SLOTS)

            first_q = lambda i: FRONT_Q + i // SLOTS
            rest(first_q(3), 3)
            rows_rest(0)
            rests(first_q, 4, GU_PAIRS)
            step_hidden(0)
            last = lambda e: (lambda i: body_q(e, i))
            with dve.Fori(0, E - 1) as e:
                rests(last(e), 0, HT_AFTER)
                hidden_rest(2 * e)
                rests(last(e), HT_AFTER, 12)
                step_hidden(2 * e + 1)
                rows_rest(e + 1)
                rests(last(e), 12, 12 + HT_AFTER)
                hidden_rest(2 * e + 1)
                rests(last(e), 12 + HT_AFTER, 24)
                step_hidden(2 * e + 2)
            rests(last(E - 1), 0, HT_AFTER)
            hidden_rest(2 * E - 2)
            rests(last(E - 1), HT_AFTER, 12)
            step_hidden(2 * E - 1)
            rests(last(E - 1), 12, 16)
            hidden_rest(2 * E - 1)

            dve.wait_ge(grow_in, 16 * 5)
            for c, buf in enumerate((xh, arena)):
                one_over_rms(4 + c)
                for i in range(TILES):
                    normalise(4 + c, buf, buf, i, fin_done)

        @block.tensor
        def _(pe):
            def products(terms):
                for part in range(3):
                    for out, lh, lr, rh, rr, start, stop in terms:
                        lhs, rhs = ((lh, rh), (lh, rr), (lr, rh))[part]
                        done = nc.tensor.matmul(out, lhs, rhs, start=start and part == 0, stop=stop and part == 2)
                return done

            def w(j, lo, n):
                return w_high[:, j, lo:lo + n], w_rest[:, j, lo:lo + n]

            def project_t(G, j, first_bank):
                pe.wait_ge(rest_done, SLOTS * G + j + 1)
                for kc in range(KC):
                    for m in range(2):
                        last = products([(bank(first_bank + m), *w(j, kc * GC + m * P, P),
                                          ut_high[:, kc * T:(kc + 1) * T], ut_rest[:, kc * T:(kc + 1) * T], kc == 0, kc == KC - 1)])
                last.then_inc(pair_used, 1)

            def attention_scores(A, s, hh):
                base = (6, 0)[s]
                for i in range(TILES):
                    lo = WIN_COL[i] * ROWS
                    last = nc.tensor.matmul(ps[:, base * BANK + i * WIN:base * BANK + (i + 1) * WIN],
                                            qz[:, hh % 2, hh // 2, i * P:(i + 1) * P], kt[:, hh // 2, lo:lo + WIN], start=True, stop=True)
                last.then_inc(s_mm, 1)

            def attention_values(A, G, s, hh):
                pe.wait_ge(exp_done, TILES * (A + 1))
                for i in range(TILES):
                    for c in range(2):
                        at = 2 * BANK + i * WIN + c * P
                        last = nc.tensor.transpose(ps[:, at:at + P], scores[:, s, i, c * P:(c + 1) * P], ident[:, :])
                last.then_inc(pt_mm, 1)
                pe.wait_ge(pt_dve, A + 1)
                pe.wait_ge(pt_act, A + 1)
                if hh >= 2:
                    pe.wait_ge(o_done, A - 1)
                if hh == 0:
                    pe.wait_ge(voff_in, 32 * (G + 1))
                for i in range(TILES):
                    row = WIN_COL[i] * ROWS
                    for c in range(2):
                        vals = v_off[:, row // P + c, hh * HD:(hh + 1) * HD] if row % P else v[:, row // P + c, hh * HD:(hh + 1) * HD]
                        last = nc.tensor.matmul(bank(4 + s)[:, i * HD:(i + 1) * HD], pt[:, s, i * WIN + c * P:i * WIN + (c + 1) * P],
                                                vals, start=c == 0, stop=c == 1)
                last.then_inc(pv_mm, 1)

            def group(G, b):
                A = GROUP * G
                project_t(G, 0, 0)
                project_t(G, 1, 2)
                pe.wait_ge(rest_done, SLOTS * G + 3)
                pe.wait_ge(h_done, TILES * (G + 1))
                for i in range(TILES):
                    for kc in range(KC):
                        at = kc * T + i * P
                        last = products([(ps[:, 4 * BANK + i * GC:4 * BANK + (i + 1) * GC], ut_high[:, at:at + P], ut_rest[:, at:at + P],
                                          *w(2, kc * GC, GC), kc == 0, kc == KC - 1)])
                last.then_inc(pair_used, 1)
                pe.wait_ge(q_done, 4 * (G + 1))
                pe.wait_ge(k_done, G + 1)
                attention_scores(A, 0, 0)
                attention_scores(A + 1, 1, 1)
                attention_values(A, G, 0, 0)
                attention_scores(A + 2, 0, 2)
                attention_values(A + 1, G, 1, 1)
                attention_scores(A + 3, 1, 3)
                attention_values(A + 2, G, 0, 2)
                attention_values(A + 3, G, 1, 3)
                pe.wait_ge(o_done, A + 4)
                for f in range(2):
                    for i in range(TILES):
                        last = nc.tensor.transpose(bank(f)[:, i * P:(i + 1) * P], o[:, i, f * P:(f + 1) * P], ident[:, :])
                    last.then_inc(ot_mm, 1)
                pe.wait_ge(otr_done, 2 * (G + 1))
                pe.wait_ge(rest_done, SLOTS * G + 4)
                for i in range(TILES):
                    if i >= 2:
                        pe.wait_ge(h_done, TILES * (G + 1) + i - 1)
                    for f in range(2):
                        last = products([(bank(4 + 2 * (i % 2) + n), ot_high[:, f, i * P:(i + 1) * P], ot_rest[:, f, i * P:(i + 1) * P],
                                          *w(3, f * D + n * BANK, BANK), f == 0, f == 1) for n in range(2)])
                    last.then_inc(wo_mm if i + 1 < TILES else pair_used, 1)

            pe.wait_ge(const_in, 32)
            pe.wait_ge(zeros_done, 2)
            for b in range(TRUNKS):
                pe.wait_ge(xs_done, TILES * (2 * b + 1))
                for kc in range(KC):
                    if kc >= 2:
                        pe.wait_ge(utr_done, KC * b + kc - 1)
                    for i in range(TILES):
                        last = nc.tensor.transpose(bank(kc % 2)[:, i * P:(i + 1) * P], arena[:, i, kc * P:(kc + 1) * P], ident[:, :])
                    last.then_inc(xt_front, 1)
                pe.wait_ge(utr_done, KC * (b + 1))
                with pe.Fori(0, GROUPS) as g:
                    group(g + GROUPS * b, b)

                pe.wait_ge(xs_done, TILES * (2 * b + 2))

                def router(kc):
                    pe.wait_ge(rt_copied, KC * b + kc + 1)
                    for i in range(TILES):
                        last = nc.tensor.matmul(bank(4 + i)[:, 0:E], kt[:, kc % 2, i * P:(i + 1) * P], rw[:, kc, :],
                                                start=kc == 0, stop=kc == KC - 1)
                    last.then_inc(rt_used, 1)

                for kc in range(KC):
                    if kc >= 2:
                        pe.wait_ge(rt_copied, KC * b + kc - 1)
                    for i in range(TILES):
                        last = nc.tensor.transpose(bank(kc % 2)[:, i * P:(i + 1) * P], arena[:, i, kc * P:(kc + 1) * P], ident[:, :])
                    last.then_inc(rt_mm, 1)
                    if kc:
                        router(kc - 1)
                router(KC - 1)

            pe.wait_ge(aff_done, 3 * TRUNKS)
            for i in range(TILES):
                last = nc.tensor.transpose(bank(0)[0:TRUNKS * E, i * P:(i + 1) * P], aff[:, i, :], ident[:, :])
            last.then_inc(afft_mm, 1)
            pe.wait_ge(top_done, 4)
            for k, table in enumerate((gv, gi)):
                last = nc.tensor.transpose(bank(1)[:, k * 2 * E:(k + 1) * 2 * E], table[:, :, :].rearrange("e a s -> e (a s)"),
                                           ident[0:TRUNKS * E, 0:TRUNKS * E])
            last.then_inc(route_mm, 1)

            def rows_t(e, before):
                pe.wait_ge(gathered, 16 * (e + 1))
                if before is not None:
                    pe.wait_ge(htr_done, before)
                for kc in range(KC):
                    last = nc.tensor.transpose(bank(6, 2)[:, kc * P:(kc + 1) * P], xg[:, kc * P:(kc + 1) * P], ident[:, :])
                last.then_inc(xt_mm, 1)

            def gate_up(s, q_of):
                for i in range(GU_PAIRS):
                    j = i % SLOTS
                    pe.wait_ge(rest_done, SLOTS * q_of(i) + j + 1)
                    for k in range(2):
                        kc = 2 * (i // 2) + k
                        at = slice(kc * P, (kc + 1) * P)
                        last = products([(bank(2 * (i % 2) + n), xt_high[:, at], xt_rest[:, at], *w(j, k * HALF + n * BANK, BANK),
                                          kc == 0, kc == KC - 1) for n in range(2)])
                    last.then_inc(pair_used, 1)

            def down(s, h, q_of, lo):
                pe.wait_ge(htr_done, s + 1)
                for i in range(lo, lo + D_PAIRS):
                    j = i % SLOTS
                    pe.wait_ge(rest_done, SLOTS * q_of(i) + j + 1)
                    for k in range(2):
                        c = 2 * (i - lo) + k
                        at = slice(c * P, (c + 1) * P)
                        last = products([(bank(4 + n), ht_high[:, at], ht_rest[:, at], *w(j, k * D + n * BANK, BANK),
                                          h == 0 and c == 0, h == 1 and c == 7) for n in range(2)])
                    last.then_inc(pair_used, 1)

            def hidden_t(s):
                pe.wait_ge(hid_done, s + 1)
                for c in range(HALF // P):
                    last = nc.tensor.transpose(bank(6, 2)[:, c * P:(c + 1) * P], hid[:, c * P:(c + 1) * P], ident[:, :])
                last.then_inc(ht_mm, 1)

            rows_t(0, None)
            pe.wait_ge(xtr_done, 1)
            gate_up(0, lambda i: FRONT_Q + i // SLOTS)
            hidden_t(0)
            with pe.Fori(0, E - 1) as e:
                at = lambda s: lambda i: body_q(e, s + i)
                gate_up(2 * e + 1, at(0))
                rows_t(e + 1, 2 * e + 1)
                pe.wait_ge(ys_done, e + 1)
                down(2 * e, 0, at(0), 8)
                pe.wait_ge(xtr_done, e + 2)
                hidden_t(2 * e + 1)
                gate_up(2 * e + 2, at(12))
                down(2 * e + 1, 1, at(0), 20)
                hidden_t(2 * e + 2)
            at = lambda s: lambda i: body_q(E - 1, s + i)
            gate_up(2 * E - 1, at(0))
            pe.wait_ge(ys_done, E)
            down(2 * E - 2, 0, at(0), 8)
            hidden_t(2 * E - 1)
            down(2 * E - 1, 1, at(0), 12)


def bias_layout(rpb):
    q, k = np.arange(P), np.arange(WIN)
    out = []
    for i in (0, 1, 3):
        qc, kcol = QCOLS * i + q // ROWS, WIN_COL[i] + k // ROWS
        start = np.clip(qc - KW // 2, 0, GRID_W - KW)
        inside = (kcol[None] >= start[:, None]) & (kcol[None] < start[:, None] + KW)
        dr = (k % ROWS)[None] - (q % ROWS)[:, None] + KH - 1
        dc = np.where(inside, kcol[None] - qc[:, None] + KW - 1, 0)
        out.append(np.where(inside[None], rpb[:, dr, dc], np.float32(MASKED)))
    return np.ascontiguousarray(np.stack(out, 2).reshape(HEADS * P, 3 * WIN))


def kernel(x_prompt, x_sample, norm_mix_g, norm_ffn_g, final_norm_g, na_w_qkv, na_rpb, na_w_o, pool_w, pool_scale,
           gla_w_in, gla_w_gate_f, gla_b_gate_f, gla_w_gate_b, gla_b_gate_b, gla_norm_g, gla_w_o,
           router_w, moe_w_gate, moe_w_up, moe_w_down):
    import concourse.bacc as bacc
    from concourse.bass_utils import run_bass_kernel_spmd

    by_column = lambda a: np.asarray(a).reshape(ROWS, GRID_W, D).transpose(1, 0, 2).reshape(T, D)
    by_row = lambda a: np.ascontiguousarray(a.reshape(GRID_W, ROWS, D).transpose(1, 0, 2).reshape(1, T, D))
    arrays = {
        "x": np.concatenate([by_column(x_prompt), by_column(x_sample)]),
        "g_mix": np.asarray(norm_mix_g).reshape(1, D),
        "g_ffn": np.asarray(norm_ffn_g).reshape(1, D),
        "g_fin": np.asarray(final_norm_g).reshape(1, D),
        "w_qkv": np.asarray(na_w_qkv)[0],
        "bias": bias_layout(np.asarray(na_rpb)[0]),
        "w_o": np.asarray(na_w_o)[0],
        "router_w": np.asarray(router_w)[0],
        "w_gate": np.asarray(moe_w_gate).reshape(E * D, F),
        "w_up": np.asarray(moe_w_up).reshape(E * D, F),
        "w_down": np.asarray(moe_w_down).reshape(E * F, D),
        "identity": np.eye(P, dtype=np.float32),
    }
    nc = bacc.Bacc("TRN2", target_bir_lowering=False, num_devices=1)
    args = {n: nc.dram_tensor(n, a.shape, mybir.dt.from_np(a.dtype), kind="ExternalInput").ap() for n, a in arrays.items()}
    y = nc.dram_tensor("y", (TRUNKS * T, D), F32, kind="ExternalOutput").ap()
    encoder_kernel(nc, *[args[n] for n in arrays], y)
    got = run_bass_kernel_spmd(nc, [arrays], core_ids=[0]).results[0]["y"]
    return by_row(got[:T]), by_row(got[T:])
```

```python
import numpy as np
import concourse.bass as bass
from concourse import mybir
from contextlib import ExitStack

F32 = mybir.dt.float32
F32R = mybir.dt.float32r
U32 = mybir.dt.uint32
ALU = mybir.AluOpType
ACT = mybir.ActivationFunctionType
AX = mybir.AxisListType

P = 128
D = 1024
T = 512
TRUNKS = 2
GRID_W = 64
ROWS = T // GRID_W
KW = 16
KH = 8
HEADS = 16
HD = D // HEADS
E = 16
CAP = 2 * T // E
F = 2048
EPS = 1e-6
MASKED = -1e30

KC = D // P
TILES = T // P
QCOLS = GRID_W // TILES
WIN = 2 * P
WIN_COL = [min(max(QCOLS * i - KW // 2, 0), GRID_W - WIN // ROWS) for i in range(TILES)]
KIND = [0, 1, 1, 2]
GROUP = 4
GROUPS = HEADS // GROUP
GC = GROUP * HD
SLOTS = 4
PAIR = 2048
HALF = F // 2
BANK = 512
FRONT_Q = TRUNKS * GROUPS
GU_PAIRS = 8
D_PAIRS = 4
OUT_JOBS = [(f"w{n}", b) for n, b in enumerate((0, 1, 5, 0, 1, 5, 0, 1))]
STAGES = {
    "pre": [("q0", 0), ("q1", 1), ("k0", 0), ("k1", 1)],
    "first": [("v0", 5), ("v1", 0), ("q0", 1), ("q1", 5), ("k0", 0), ("k1", 1), ("t0", 5), ("t1", 0)],
    "inner": [("v0", 1), ("v1", 5), *OUT_JOBS, ("q0", 5), ("q1", 0), ("k0", 1), ("t0", 5), ("t1", 0), ("k1", 1)],
    "last": [("v0", 1), ("v1", 5), *OUT_JOBS, ("t0", 5), ("t1", 0),
             *[(f"o{n}", b) for n, b in enumerate((1, 5, 0, 1, 5, 0, 1, 5))]],
}
PAIRS = [("q", 0), ("k", 0), ("v", 0), ("q", 1), ("k", 1), ("v", 1), ("w", 0), ("q", 2), ("k", 2), ("v", 2), ("w", 1),
         ("q", 3), ("k", 3), ("v", 3), ("w", 2), ("w", 3)]
SLOT = {"pre": dict(q=0, k=1), "first": dict(v=2, q=3, k=0), "inner": dict(v=1, w=2, q=3, k=0), "last": dict(v=1, w=2, o=3)}
FRONT_PAIRS = TRUNKS * len(PAIRS)
NORM_BANKS = (2, 3, 6, 7)
K_BANK = 1


def stage_name(g):
    return {0: "first", GROUPS - 1: "last"}.get(g, "inner") if isinstance(g, int) else "inner"


def jobs_before(b, g, bank):
    pre, first, inner, last = (sum(k == bank for _, k in STAGES[n]) for n in ("pre", "first", "inner", "last"))
    at = b * (pre + first + (GROUPS - 2) * inner + last)
    if g is None:
        return at
    return at + pre + {"first": 0, "inner": first + (g - 1) * inner, "last": first + (GROUPS - 2) * inner}[stage_name(g)]


def turn(b, g, job):
    jobs = STAGES["pre" if g is None else stage_name(g)]
    at = [n for n, _ in jobs].index(job)
    bank = jobs[at][1]
    return bank, jobs_before(b, g, bank) + sum(k == bank for _, k in jobs[:at])


HT_AFTER = 6


def encoder_kernel(nc, x, g_mix, g_ffn, g_fin, w_qkv, bias, w_o, router_w, w_gate, w_up, w_down, identity, y):
    h_dram = nc.dram_tensor("h_rows", [TRUNKS * T, D], F32).ap()
    u_dram = nc.dram_tensor("u_rows", [TRUNKS * T, D], F32).ap()
    wqkv_v = w_qkv.rearrange("(k p) n -> p k n", p=P)
    wo_v = w_o.rearrange("(k p) n -> p k n", p=P)

    with ExitStack() as ctx:
        def sb(name, shape, dt=F32):
            return ctx.enter_context(nc.sbuf_tensor(name, shape, dt))

        def sem(name):
            return ctx.enter_context(nc.semaphore(name))

        raw = sb("raw", [P, SLOTS, PAIR])
        w_high = sb("w_high", [P, SLOTS, PAIR], F32R)
        w_rest = sb("w_rest", [P, SLOTS, PAIR], F32R)
        xh = sb("xh", [P, TILES, D])
        arena = sb("arena", [P, TILES, D])
        ut_high = sb("ut_high", [P, KC * T], F32R)
        ut_rest = sb("ut_rest", [P, KC * T], F32R)
        early = sb("early", [P, TILES * D])
        v = sb("v", [P, TILES, GC])
        v_off = sb("v_off", [P, TILES - 1, GC])
        bias_sb = sb("bias_sb", [P, 2, 3, WIN])
        ot_high = sb("ot_high", [P, 2, T], F32R)
        ot_rest = sb("ot_rest", [P, 2, T], F32R)
        grow = sb("grow", [P, D])
        g_col = sb("g_col", [P, KC])
        ident = sb("ident", [P, P])
        rw = sb("rw", [P, KC, E])
        aff = sb("aff", [P, TILES, TRUNKS * E])
        lg = sb("lg", [P, TILES, E])
        ssq = sb("ssq", [P, 24])
        var = sb("var", [P, 24])
        sdev = sb("sdev", [P, 24])
        rstd = sb("rstd", [P, 24])
        newt = sb("newt", [P, 3, 24])
        mx = sb("mx", [P, 2, TILES])
        nmx = sb("nmx", [P, 2, TILES])
        psum_row = sb("psum_row", [P, 2, TILES])
        rinv = sb("rinv", [P, 2, TILES])
        lstat = sb("lstat", [P, TRUNKS, 3, TILES])
        topv = sb("topv", [TRUNKS * E, CAP])
        topi = sb("topi", [TRUNKS * E, CAP], U32)
        topt = sb("topt", [TRUNKS * E, 3, CAP], U32)
        gv = sb("gv", [TRUNKS * E, 2, CAP])
        gi = sb("gi", [TRUNKS * E, 2, CAP])
        gate_w = sb("gate_w", [P, E])
        rows = sb("rows", [P, E], U32)

        early_t = early[:, :].rearrange("p (i d) -> p i d", i=TILES)
        qz = early[:, 0:4 * T].rearrange("p (a m t) -> p a m t", a=2, m=2)
        kt = early[:, 4 * T:6 * T].rearrange("p (m t) -> p m t", m=2)
        o = early[:, 6 * T:8 * T].rearrange("p (i n) -> p i n", i=TILES)
        scores = arena[:, 3, :].rearrange("p (i k) -> p i k", i=TILES)
        pt = arena[:, 2, :]
        rt = v[:, :, :].rearrange("p (a b) n -> p a (b n)", a=2)
        affw = arena[0:TRUNKS * E, 0, 0:T]
        xg = xh[:, 0, :]
        silu = xh[:, 1, :]
        hid = xh[:, 2, :]
        ys = xh[:, 3, :]
        xt_high = ut_high[:, 0:D]
        xt_rest = ut_rest[:, 0:D]
        ht_high = ut_high[:, D:2 * D]
        ht_rest = ut_rest[:, D:2 * D]

        ps = ctx.enter_context(nc.psum_tensor("ps", [P, 8 * BANK], F32))

        def bank(b, n=1):
            return ps[:, b * BANK:(b + n) * BANK]

        const_in = sem("const_in")
        bias_in = [sem(f"bias_in{s}") for s in range(2)]
        xe_in = [[sem(f"xe_in{b}{c}") for c in "ab"] for b in range(TRUNKS)]
        xh_in = sem("xh_in")
        grow_in = sem("grow_in")
        full = {k: sem(f"full{k}") for k in (0, 1, 5)}
        free = {k: sem(f"free{k}") for k in (0, 1, 5)}
        raw_in = [sem(f"raw_in{j}") for j in range(SLOTS)]
        voff_in = sem("voff_in")
        h_out = sem("h_out")
        u_out = sem("u_out")
        gathered = sem("gathered")
        scattered = sem("scattered")
        ys_free = sem("ys_free")
        h_in = [sem(f"h_in{c}") for c in range(TRUNKS)]
        y_out = sem("y_out")
        high_done = sem("high_done")
        rest_done = sem("rest_done")
        pair_used = sem("pair_used")
        zeros_done = sem("zeros_done")
        ssq_done = sem("ssq_done")
        var_done = sem("var_done")
        sdev_done = sem("sdev_done")
        norm_step = sem("norm_step")
        xe_done = sem("xe_done")
        xs_done = sem("xs_done")
        xt_front = sem("xt_front")
        uth_done = sem("uth_done")
        utr_done = sem("utr_done")
        s_mm = sem("s_mm")
        max_done = sem("max_done")
        nmx_done = sem("nmx_done")
        exp_done = sem("exp_done")
        pt_mm = sem("pt_mm")
        pt_act, pt_dve = sem("pt_act"), sem("pt_dve")
        pv_mm = sem("pv_mm")
        rinv_done = sem("rinv_done")
        o_done = sem("o_done")
        oth_done = sem("oth_done")
        rt_mm = sem("rt_mm")
        rt_copied = sem("rt_copied")
        rt_used = sem("rt_used")
        lg_step = sem("lg_step")
        lexp_done = sem("lexp_done")
        aff_done = sem("aff_done")
        afft_mm = sem("afft_mm")
        top_step = sem("top_step")
        top_done = sem("top_done")
        route_mm = sem("route_mm")
        route_done = sem("route_done")
        xt_mm, xth_done, xtr_done = sem("xt_mm"), sem("xth_done"), sem("xtr_done")
        silu_done, hid_done = sem("silu_done"), sem("hid_done")
        ht_mm, hth_done, htr_done = sem("ht_mm"), sem("hth_done"), sem("htr_done")
        ys_done = sem("ys_done")
        fin_done = sem("fin_done")

        block = ctx.enter_context(nc.Block())

        def body_q(e, i):
            return FRONT_Q + GU_PAIRS // SLOTS + (2 * (GU_PAIRS + D_PAIRS) // SLOTS) * e + i // SLOTS

        def pairs_before(e):
            return SLOTS * (body_q(e, 0) - FRONT_Q)

        def wait_full(eng, b, g, job):
            bank, before = turn(b, g, job)
            eng.wait_ge(full[bank], before + 1)
            return bank

        def wait_copied(eng, b, g, job):
            bank, before = turn(b, g, job)
            eng.wait_ge(free[bank], before + 1)

        def head_count(b, g):
            return HEADS * b + GROUP * g

        @block.sync
        def _(sp):
            sp.dma_start(ident[:, :], identity).then_inc(const_in, 16)
            sp.dma_start(g_col[:, :], g_mix).then_inc(const_in, 16)
            sp.dma_start(rw[:, :, :], router_w.rearrange("(k p) e -> p k e", p=P)).then_inc(const_in, 16)

            def load(q, j, src):
                if not (isinstance(q, int) and q == 0):
                    sp.wait_ge(rest_done, SLOTS * (q - 1) + j + 1)
                sp.dma_start(raw[:, j, :].rearrange("p (k n) -> p k n", k=src.shape[1]), src).then_inc(raw_in[j], 16)

            def load_gate_up(e, h, q_of, lo=0, hi=GU_PAIRS):
                for jj in range(lo, hi):
                    src = (w_gate, w_up)[jj % 2]
                    rows_ = src[bass.ds(e * D + (jj // 2) * 2 * P, 2 * P), h * HALF:(h + 1) * HALF]
                    load(q_of(jj), jj % SLOTS, rows_.rearrange("(k p) n -> p k n", p=P))

            def load_down(e, h, q_of):
                for jj in range(D_PAIRS):
                    rows_ = w_down[bass.ds(e * F + h * HALF + jj * 2 * P, 2 * P), :]
                    load(q_of(jj), jj % SLOTS, rows_.rearrange("(k p) n -> p k n", p=P))

            first_q = lambda i: FRONT_Q + i // SLOTS

            def load_nth(n):
                if n >= FRONT_PAIRS:
                    return load_gate_up(0, 0, first_q, n - FRONT_PAIRS, n - FRONT_PAIRS + 1)
                what, g = PAIRS[n % len(PAIRS)]
                if what == "w":
                    src = wo_v[:, 2 * g:2 * g + 2, :]
                else:
                    c = "qkv".index(what) * D + g * GC
                    src = wqkv_v[:, :, c:c + GC]
                load(n // SLOTS, n % SLOTS, src)

            def load_bias(A):
                if A >= TRUNKS * HEADS:
                    return
                if A >= 2:
                    sp.wait_ge(max_done, TILES * (A - 1))
                sp.dma_start(bias_sb[:, A % 2, :, :].rearrange("p a k -> p (a k)"),
                             bias[(A % HEADS) * P:(A % HEADS + 1) * P, :]).then_inc(bias_in[A % 2], 16)

            for c, (lo, hi) in enumerate(((0, 3), (3, 4))):
                sp.dma_start(early_t[:, lo:hi, :], x[lo * P:hi * P, :].rearrange("(i p) d -> p i d", p=P)).then_inc(xe_in[0][c], 16)
            for n in range(SLOTS):
                load_nth(n)
            load_bias(0)
            load_bias(1)
            for n in range(SLOTS, 2 * SLOTS):
                load_nth(n)
            for b in range(TRUNKS):
                n = len(PAIRS) * b + 2 * SLOTS
                load_nth(n)
                for g in range(GROUPS):
                    skip = {0: 2, GROUPS - 1: 3}.get(g)
                    for hh in range(GROUP):
                        load_bias(head_count(b, g) + hh + 2)
                        if hh != skip:
                            n += 1
                            load_nth(n)
                n += 1
                load_nth(n)
            with sp.Fori(0, E - 1) as e:
                at = lambda s: lambda i: body_q(e, s + i)
                load_gate_up(e, 1, at(0))
                load_down(e, 0, at(GU_PAIRS))
                load_gate_up(e + 1, 0, at(GU_PAIRS + D_PAIRS))
                load_down(e, 1, at(2 * GU_PAIRS + D_PAIRS))
            at = lambda s: lambda i: body_q(E - 1, s + i)
            load_gate_up(E - 1, 1, at(0))
            load_down(E - 1, 0, at(GU_PAIRS))
            load_down(E - 1, 1, at(GU_PAIRS + D_PAIRS))

            sp.wait_ge(scattered, 16 * E)
            sp.dma_start(xh[:, :, :], h_dram[0:T, :].rearrange("(i p) d -> p i d", p=P)).then_inc(h_in[0], 16)
            sp.dma_start(arena[:, :, :], h_dram[T:2 * T, :].rearrange("(i p) d -> p i d", p=P)).then_inc(h_in[1], 16)
            for c, buf in enumerate((xh, arena)):
                for i in range(TILES):
                    sp.wait_ge(fin_done, c * TILES + i + 1)
                    sp.dma_start(y[c * T + i * P:c * T + (i + 1) * P, :], buf[:, i, :]).then_inc(y_out, 16)
            sp.wait_ge(y_out, 16 * TRUNKS * TILES)

        @block.gpsimd
        def _(pool):
            def load_grow(g):
                pool.dma_start(grow[:, :], g.broadcast_to([P, D])).then_inc(grow_in, 16)

            def rows_of(buf, dram, b, lo=0, hi=TILES):
                return buf[:, lo:hi, :], dram[b * T + lo * P:b * T + hi * P, :].rearrange("(i p) d -> p i d", p=P)

            pool.dma_start(*rows_of(xh, x, 0)).then_inc(xh_in, 16)
            load_grow(g_ffn)
            for b in range(TRUNKS):
                pool.wait_ge(xt_front, KC * (b + 1))
                nc.gpsimd.memset(qz[HD:P, 0, :, :], 0.0).then_inc(zeros_done, 1)
                nc.gpsimd.memset(qz[0:HD, 1, :, :], 0.0).then_inc(zeros_done, 1)
                if b:
                    pool.wait_ge(u_out, 16 * b)
                    pool.wait_ge(h_out, 16 * b)
                    pool.dma_start(*rows_of(xh, x, b)).then_inc(xh_in, 16)
                if b + 1 < TRUNKS:
                    pool.wait_ge(s_mm, HEADS * (b + 1))
                    pool.dma_start(*rows_of(early_t, x, b + 1, 0, 3)).then_inc(xe_in[b + 1][0], 16)
                    wait_full(pool, b, GROUPS - 1, "t1")
                    pool.dma_start(*rows_of(early_t, x, b + 1, 3, 4)).then_inc(xe_in[b + 1][1], 16)
                for k in full:
                    pool.wait_ge(free[k], jobs_before(b + 1, None, k))
                out, src = rows_of(xh, h_dram, b)
                pool.dma_start(src, out).then_inc(h_out, 16)
                pool.wait_ge(xs_done, TILES * (b + 1))
                out, src = rows_of(arena, u_dram, b)
                pool.dma_start(src, out).then_inc(u_out, 16)
            load_grow(g_fin)

            def gather(e):
                pool.indirect_dma_start(xg, None, u_dram, bass.IndirectOffsetOnAxis(ap=rows[:, e:e + 1], axis=0)).then_inc(gathered, 16)

            pool.sem_inc(ys_free, 1)
            pool.wait_ge(u_out, 16 * TRUNKS)
            pool.wait_ge(h_out, 16 * TRUNKS)
            pool.wait_ge(route_done, 1)
            gather(0)
            for e in range(E):
                if e + 1 < E:
                    pool.wait_ge(xt_mm, e + 1)
                    gather(e + 1)
                if e:
                    pool.wait_ge(scattered, 16 * e)
                    pool.sem_inc(ys_free, 1)
                pool.wait_ge(ys_done, e + 2)
                pool.indirect_dma_start(h_dram, bass.IndirectOffsetOnAxis(ap=rows[:, e:e + 1], axis=0), ys, None,
                                        compute_op=ALU.add).then_inc(scattered, 16)
            pool.wait_ge(scattered, 16 * E)

        @block.scalar
        def _(act):
            def high(q, j):
                act.wait_ge(raw_in[j], 16 * (q + 1))
                nc.scalar.copy(w_high[:, j, :], raw[:, j, :]).then_inc(high_done, 1)

            def squares(c, src, junk):
                for i in range(TILES):
                    nc.scalar.activation(junk(i), src[:, i, :], ACT.Square, accum_out=ssq[:, TILES * c + i:TILES * c + i + 1]).then_inc(ssq_done, 1)

            def root(c):
                act.wait_ge(var_done, c + 1)
                nc.scalar.activation(sdev[:, TILES * c:TILES * (c + 1)], var[:, TILES * c:TILES * (c + 1)], ACT.Sqrt).then_inc(sdev_done, 1)

            def exponentials(A, hh):
                act.wait_ge(nmx_done, A + hh + 1)
                for i in range(TILES):
                    nc.scalar.activation(scores[:, i, :], scores[:, i, :], ACT.Exp, bias=nmx[:, hh % 2, i:i + 1],
                                         accum_out=psum_row[:, hh % 2, i:i + 1]).then_inc(exp_done, 1)

            def copy_pt(A, hh):
                act.wait_ge(pt_mm, A + hh + 1)
                nc.scalar.copy(pt[:, 512:1024], bank(3)).then_inc(pt_act, 1)

            def copy_v(b, g, part):
                k = wait_full(act, b, g, f"v{part}")
                nc.scalar.copy(v[:, 2 * part:2 * part + 2, :].rearrange("p i n -> p (i n)"), bank(k)).then_inc(free[k], 1)

            def shift_v(b, g):
                wait_copied(act, b, g, "v0")
                wait_copied(act, b, g, "v1")
                act.dma_start(v_off[0:HD, :, :], v[HD:P, 0:TILES - 1, :]).then_inc(voff_in, 16)
                act.dma_start(v_off[HD:P, :, :], v[0:HD, 1:TILES, :]).then_inc(voff_in, 16)

            def copy_q(b, g, m):
                k = wait_full(act, b, g, f"q{m}")
                nc.scalar.mul(qz[0:HD, 0, m, :], bank(k)[0:HD, :], HD ** -0.5)
                nc.scalar.mul(qz[HD:P, 1, m, :], bank(k)[HD:P, :], HD ** -0.5).then_inc(free[k], 1)

            def split_ot(b, g):
                for f in range(2):
                    k = wait_full(act, b, g, f"t{f}")
                    nc.scalar.copy(ot_high[:, f, :], bank(k)).then_inc(oth_done, 1)

            def next_high(b, g, what, last_job, q):
                wait_full(act, b, g, last_job)
                high(q, SLOT["pre" if g is None else stage_name(g)][what])

            def first_norm(b):
                for part in xe_in[b]:
                    act.wait_ge(part, 16)
                squares(b, early_t, lambda i: arena[:, i, :])
                root(b)

            def split_x(b):
                for kc in range(KC):
                    act.wait_ge(xt_front, KC * b + kc + 1)
                    nc.scalar.activation(ut_high[:, kc * T:(kc + 1) * T], bank(NORM_BANKS[kc % 4]), ACT.Copy,
                                         scale=g_col[:, kc:kc + 1]).then_inc(uth_done, 1)

            def before_groups(b):
                copy_q(b, None, 0)
                copy_q(b, None, 1)
                next_high(b, None, "q", "q1", SLOTS * b + 1)

            def second_norm(b):
                for k in full:
                    act.wait_ge(free[k], jobs_before(b + 1, None, k))
                squares(TRUNKS + b, xh, lambda i: arena[:, i, :])
                root(TRUNKS + b)

            def router(b):
                for kc in range(KC):
                    act.wait_ge(rt_mm, KC * b + kc + 1)
                    if kc >= 2:
                        act.wait_ge(rt_used, KC * b + kc - 1)
                    nc.scalar.copy(rt[:, kc % 2, :], bank(2 + kc % 2)).then_inc(rt_copied, 1)
                act.wait_ge(lg_step, 2 * (b + 1))
                nc.scalar.activation(lg[:, :, :], lg[:, :, :], ACT.Exp).then_inc(lexp_done, 1)

            def group(b, g):
                A = head_count(b, g)
                kind = stage_name(g)
                at = SLOTS * b + g + 1
                exponentials(A, 0)
                act.wait_ge(full[K_BANK], jobs_before(b, g, K_BANK))
                high(at, 1 if kind == "first" else 0)
                copy_v(b, g, 0)
                copy_pt(A, 0)
                exponentials(A, 1)
                copy_v(b, g, 1)
                shift_v(b, g)
                next_high(b, g, "v", "v1", at)
                copy_pt(A, 1)
                exponentials(A, 2)
                if kind != "first":
                    next_high(b, g, "w", "w7", at)
                copy_pt(A, 2)
                exponentials(A, 3)
                if kind == "last":
                    copy_pt(A, 3)
                else:
                    copy_q(b, g, 0)
                    if kind == "inner":
                        copy_pt(A, 3)
                    copy_q(b, g, 1)
                    next_high(b, g, "q", "q1", at)
                    if kind == "first":
                        copy_pt(A, 3)
                split_ot(b, g)

            act.sem_inc(ys_done, 1)
            first_norm(0)
            high(0, 0)
            act.wait_ge(const_in, 16 * 3)
            split_x(0)
            for j in range(1, SLOTS):
                high(0, j)
            before_groups(0)
            for b in range(TRUNKS):
                group(b, 0)
                with act.Fori(1, GROUPS - 1) as g:
                    group(b, g)
                group(b, GROUPS - 1)
                if b + 1 < TRUNKS:
                    first_norm(b + 1)
                next_high(b, GROUPS - 1, "o", "o7", SLOTS * (b + 1))
                if b + 1 < TRUNKS:
                    split_x(b + 1)
                second_norm(b)
                if b + 1 < TRUNKS:
                    before_groups(b + 1)
                router(b)

            def step_silu(s, used_by_gate_up):
                act.wait_ge(pair_used, used_by_gate_up)
                nc.scalar.activation(silu, bank(0, 2), ACT.Silu).then_inc(silu_done, 1)

            def rows_high(e):
                act.wait_ge(xt_mm, e + 1)
                nc.scalar.copy(xt_high, bank(6, 2)).then_inc(xth_done, 1)

            def hidden_high(s):
                act.wait_ge(ht_mm, s + 1)
                nc.scalar.copy(ht_high, bank(6, 2)).then_inc(hth_done, 1)

            def result(e, used_by_down):
                act.wait_ge(pair_used, used_by_down)
                act.wait_ge(ys_free, e + 1)
                nc.scalar.activation(ys, bank(4, 2), ACT.Copy, scale=gate_w[:, bass.ds(e, 1)]).then_inc(ys_done, 1)

            def highs(q_of, lo, hi):
                for i in range(lo, hi):
                    act.wait_ge(pair_used, SLOTS * (q_of(i) - FRONT_Q - 1) + i % SLOTS + 1)
                    high(q_of(i), i % SLOTS)

            first_q = lambda i: FRONT_Q + i // SLOTS
            rows_high(0)
            highs(first_q, SLOTS, GU_PAIRS)
            step_silu(0, GU_PAIRS)
            last = lambda e: (lambda i: body_q(e, i))
            highs(last(0), 0, HT_AFTER)
            hidden_high(0)
            with act.Fori(0, E - 1) as e:
                highs(last(e), HT_AFTER, 12)
                step_silu(2 * e + 1, pairs_before(e) + GU_PAIRS)
                rows_high(e + 1)
                highs(last(e), 12, 12 + HT_AFTER)
                hidden_high(2 * e + 1)
                highs(last(e), 12 + HT_AFTER, 24)
                step_silu(2 * e + 2, pairs_before(e) + 2 * GU_PAIRS + D_PAIRS)
                highs(last(e + 1), 0, HT_AFTER)
                hidden_high(2 * e + 2)
                result(e, pairs_before(e) + 2 * (GU_PAIRS + D_PAIRS))
            highs(last(E - 1), HT_AFTER, 12)
            step_silu(2 * E - 1, pairs_before(E - 1) + GU_PAIRS)
            highs(last(E - 1), 12, 16)
            hidden_high(2 * E - 1)
            result(E - 1, pairs_before(E - 1) + GU_PAIRS + 2 * D_PAIRS)

            for c, buf in enumerate((xh, arena)):
                act.wait_ge(h_in[c], 16)
                squares(4 + c, buf, lambda i: raw[:, 2 * c + i // 2, (i % 2) * D:(i % 2 + 1) * D])
                root(4 + c)

        @block.vector
        def _(dve):
            def rest(q, j):
                dve.wait_ge(high_done, SLOTS * q + j + 1)
                nc.vector.tensor_tensor(w_rest[:, j, :], raw[:, j, :], w_high[:, j, :].bitcast(F32), ALU.subtract).then_inc(rest_done, 1)

            def one_over_rms(c):
                cols = slice(TILES * c, TILES * (c + 1))
                dve.wait_ge(ssq_done, TILES * (c + 1))
                nc.vector.tensor_scalar(var[:, cols], ssq[:, cols], 1.0 / D, EPS, ALU.mult, ALU.add).then_inc(var_done, 1)
                dve.wait_ge(sdev_done, c + 1)
                n = 5 * c

                nc.vector.reciprocal(newt[:, 0, cols], sdev[:, cols]).then_inc(norm_step, 1)
                dve.wait_ge(norm_step, n + 1)
                nc.vector.tensor_tensor(newt[:, 1, cols], newt[:, 0, cols], newt[:, 0, cols], ALU.mult).then_inc(norm_step, 1)
                dve.wait_ge(norm_step, n + 2)
                nc.vector.tensor_tensor(newt[:, 2, cols], newt[:, 1, cols], var[:, cols], ALU.mult).then_inc(norm_step, 1)
                dve.wait_ge(norm_step, n + 3)
                nc.vector.tensor_scalar(newt[:, 1, cols], newt[:, 2, cols], -0.5, 1.5, ALU.mult, ALU.add).then_inc(norm_step, 1)
                dve.wait_ge(norm_step, n + 4)
                nc.vector.tensor_tensor(rstd[:, cols], newt[:, 0, cols], newt[:, 1, cols], ALU.mult).then_inc(norm_step, 1)
                dve.wait_ge(norm_step, n + 5)

            def normalise(c, dst, src, i, done):
                nc.vector.scalar_tensor_tensor(out=dst[:, i, :], in0=src[:, i, :], scalar=rstd[:, TILES * c + i:TILES * c + i + 1],
                                               in1=grow[:, :], op0=ALU.mult, op1=ALU.mult).then_inc(done, 1)

            def biased(A, b, g, hh):
                dve.wait_ge(s_mm, A + hh + 1)
                dve.wait_ge(bias_in[hh % 2], 16 * (HEADS // 2 * b + GROUP // 2 * g + hh // 2 + 1))
                nc.vector.memset(nmx[:, hh % 2, :], 0.0)
                for i in range(TILES):
                    nc.vector.tensor_tensor_reduce(out=scores[:, i, :], in0=ps[:, 6 * BANK + i * WIN:6 * BANK + (i + 1) * WIN],
                                                   in1=bias_sb[:, hh % 2, KIND[i], :], scale=1.0, scalar=-3e38, op0=ALU.add,
                                                   op1=ALU.max, accum_out=mx[:, hh % 2, i:i + 1]).then_inc(max_done, 1)
                dve.wait_ge(max_done, TILES * (A + hh + 1))
                nc.vector.tensor_scalar(nmx[:, hh % 2, :], mx[:, hh % 2, :], -1.0, None, ALU.mult).then_inc(nmx_done, 1)

            def copy_pt(A, hh):
                dve.wait_ge(pt_mm, A + hh + 1)
                nc.vector.tensor_copy(pt[:, 0:512], bank(2)).then_inc(pt_dve, 1)

            def output(A, hh):
                s = hh % 2
                nc.vector.reciprocal(rinv[:, s, :], psum_row[:, s, :]).then_inc(rinv_done, 1)
                dve.wait_ge(rinv_done, A + hh + 1)
                dve.wait_ge(pv_mm, A + hh + 1)
                nc.vector.tensor_tensor(o[:, :, hh * HD:(hh + 1) * HD],
                                        bank(4)[:, 0:TILES * HD].rearrange("p (i n) -> p i n", i=TILES),
                                        rinv[:, s, :].rearrange("p (i a) -> p i a", a=1).broadcast_to([P, TILES, HD]), ALU.mult).then_inc(o_done, 1)

            def copy_k(b, g, m):
                k = wait_full(dve, b, g, f"k{m}")
                nc.vector.tensor_copy(kt[:, m, :], bank(k)).then_inc(free[k], 1)

            def split_ot(b, g):
                for f in range(2):
                    k, _ = turn(b, g, f"t{f}")
                    dve.wait_ge(oth_done, 2 * (GROUPS * b + g) + f + 1)
                    nc.vector.tensor_tensor(ot_rest[:, f, :], bank(k), ot_high[:, f, :].bitcast(F32), ALU.subtract).then_inc(free[k], 1)

            def add_out(b, g, what, lo, hi):
                for n in range(lo, hi):
                    k = wait_full(dve, b, g, f"{what}{n}")
                    part = xh[:, n // 2, (n % 2) * BANK:(n % 2 + 1) * BANK]
                    nc.vector.tensor_tensor(part, bank(k), part, ALU.add).then_inc(free[k], 1)

            def first_norm(b):
                one_over_rms(b)
                for i in range(TILES):
                    nc.vector.tensor_scalar(early_t[:, i, :], early_t[:, i, :], rstd[:, TILES * b + i:TILES * b + i + 1], None,
                                            ALU.mult).then_inc(xe_done, 1)

            def split_x(b):
                for kc in range(KC):
                    dve.wait_ge(uth_done, KC * b + kc + 1)
                    nc.vector.scalar_tensor_tensor(out=ut_rest[:, kc * T:(kc + 1) * T], in0=bank(NORM_BANKS[kc % 4]),
                                                   scalar=g_col[:, kc:kc + 1], in1=ut_high[:, kc * T:(kc + 1) * T].bitcast(F32),
                                                   op0=ALU.mult, op1=ALU.subtract).then_inc(utr_done, 1)

            def before_groups(b):
                rest(SLOTS * b + 1, 0)
                copy_k(b, None, 0)
                copy_k(b, None, 1)

            def group(b, g):
                A = head_count(b, g)
                kind = stage_name(g)
                at = SLOTS * b + g + 1
                biased(A, b, g, 0)
                rest(at, 1 if kind == "first" else 0)
                copy_pt(A, 0)
                biased(A, b, g, 1)
                rest(at, SLOT[kind]["v"])
                if kind == "first":
                    output(A, 0)
                    copy_pt(A, 1)
                    biased(A, b, g, 2)
                    output(A, 1)
                    copy_pt(A, 2)
                    biased(A, b, g, 3)
                    rest(at, SLOT[kind]["q"])
                    copy_k(b, g, 0)
                    output(A, 2)
                    copy_pt(A, 3)
                    copy_k(b, g, 1)
                    output(A, 3)
                    split_ot(b, g)
                    return
                cuts = (0, 4, 8, 8) if kind == "inner" else (0, 2, 5, 8)
                add_out(b, g, "w", cuts[0], cuts[1])
                output(A, 0)
                copy_pt(A, 1)
                biased(A, b, g, 2)
                add_out(b, g, "w", cuts[1], cuts[2])
                if kind == "inner":
                    rest(at, SLOT[kind]["w"])
                output(A, 1)
                copy_pt(A, 2)
                biased(A, b, g, 3)
                if kind == "last":
                    add_out(b, g, "w", cuts[2], cuts[3])
                    rest(at, SLOT[kind]["w"])
                output(A, 2)
                copy_pt(A, 3)
                if kind == "inner":
                    rest(at, SLOT[kind]["q"])
                    output(A, 3)
                    copy_k(b, g, 0)
                    split_ot(b, g)
                    copy_k(b, g, 1)
                else:
                    output(A, 3)
                    split_ot(b, g)
                    add_out(b, g, "o", 0, 8)

            first_norm(0)
            rest(0, 0)
            split_x(0)
            for j in range(1, SLOTS):
                rest(0, j)
            before_groups(0)
            for b in range(TRUNKS):
                dve.wait_ge(xh_in, 16 * (b + 1))
                if b:
                    dve.wait_ge(u_out, 16 * b)
                group(b, 0)
                with dve.Fori(1, GROUPS - 1) as g:
                    group(b, g)
                group(b, GROUPS - 1)
                if b + 1 < TRUNKS:
                    first_norm(b + 1)
                rest(SLOTS * (b + 1), SLOT["last"]["o"])
                if b + 1 < TRUNKS:
                    split_x(b + 1)

                one_over_rms(TRUNKS + b)
                dve.wait_ge(grow_in, 16)
                for i in range(TILES):
                    normalise(TRUNKS + b, arena, xh, i, xs_done)
                if b + 1 < TRUNKS:
                    before_groups(b + 1)
                dve.wait_ge(rt_used, KC * (b + 1))
                logits = bank(4, 4).rearrange("p (i n) -> p i n", i=TILES)[:, :, 0:E]
                spread = lambda a: a.rearrange("p (i a) -> p i a", a=1).broadcast_to([P, TILES, E])
                nc.vector.tensor_reduce(lstat[:, b, 0, :], logits, AX.X, ALU.max).then_inc(lg_step, 1)
                dve.wait_ge(lg_step, 2 * b + 1)
                nc.vector.tensor_tensor(lg[:, :, :], logits, spread(lstat[:, b, 0, :]), ALU.subtract).then_inc(lg_step, 1)
                dve.wait_ge(lexp_done, b + 1)
                nc.vector.tensor_reduce(lstat[:, b, 1, :], lg[:, :, :], AX.X, ALU.add).then_inc(aff_done, 1)
                dve.wait_ge(aff_done, 3 * b + 1)
                nc.vector.reciprocal(lstat[:, b, 2, :], lstat[:, b, 1, :]).then_inc(aff_done, 1)
                dve.wait_ge(aff_done, 3 * b + 2)
                nc.vector.tensor_tensor(aff[:, :, b * E:(b + 1) * E], lg[:, :, :], spread(lstat[:, b, 2, :]), ALU.mult).then_inc(aff_done, 1)
                dve.wait_ge(aff_done, 3 * b + 3)

            count = 0

            def link(instruction):
                nonlocal count
                count += 1
                instruction.then_inc(top_step, 1)
                dve.wait_ge(top_step, count)

            dve.wait_ge(u_out, 32)
            dve.wait_ge(afft_mm, 1)
            link(nc.vector.tensor_copy(affw.rearrange("e (r i c) -> e r i c", r=ROWS, i=TILES),
                                       bank(0)[0:TRUNKS * E, :].rearrange("e (i c r) -> e r i c", i=TILES, r=ROWS)))
            for k in range(CAP // 8):
                best = topv[:, 8 * k:8 * k + 8]
                link(nc.vector.max(best, affw))
                link(nc.vector.max_index(topi[:, 8 * k:8 * k + 8], best, affw))
                if k + 1 < CAP // 8:
                    link(nc.vector.match_replace(affw, best, affw, -1.0))
            link(nc.vector.tensor_scalar(topt[:, 0, :], topi[:, :], GRID_W - 1, ROWS.bit_length() - 1, ALU.bitwise_and, ALU.logical_shift_left))
            link(nc.vector.tensor_scalar(topt[:, 1, :], topi[:, :], GRID_W.bit_length() - 1, None, ALU.logical_shift_right))
            link(nc.vector.tensor_tensor(topt[:, 2, :], topt[:, 0, :], topt[:, 1, :], ALU.bitwise_or))
            for k in range(2):
                nc.vector.tensor_copy(gv[:, k, :], topv[:, :]).then_inc(top_done, 1)
                nc.vector.tensor_copy(gi[:, k, :], topt[:, 2, :]).then_inc(top_done, 1)
            dve.wait_ge(route_mm, 1)
            link(nc.vector.tensor_copy(gate_w[0:CAP, :], bank(1)[0:CAP, 0:E]))
            link(nc.vector.tensor_copy(gate_w[CAP:P, :], bank(1)[CAP:P, E:2 * E]))
            link(nc.vector.tensor_copy(rows[0:CAP, :], bank(1)[0:CAP, 2 * E:3 * E]))
            nc.vector.tensor_scalar(rows[CAP:P, :], bank(1)[CAP:P, 3 * E:4 * E], float(T), None, ALU.add).then_inc(route_done, 1)

            def step_hidden(s):
                dve.wait_ge(silu_done, s + 1)
                nc.vector.tensor_tensor(hid, bank(2, 2), silu, ALU.mult).then_inc(hid_done, 1)

            def rows_rest(e):
                dve.wait_ge(xth_done, e + 1)
                nc.vector.tensor_tensor(xt_rest, bank(6, 2), xt_high.bitcast(F32), ALU.subtract).then_inc(xtr_done, 1)

            def hidden_rest(s):
                dve.wait_ge(hth_done, s + 1)
                nc.vector.tensor_tensor(ht_rest, bank(6, 2), ht_high.bitcast(F32), ALU.subtract).then_inc(htr_done, 1)

            def rests(q_of, lo, hi):
                for i in range(lo, hi):
                    rest(q_of(i), i % SLOTS)

            first_q = lambda i: FRONT_Q + i // SLOTS
            rows_rest(0)
            rests(first_q, SLOTS, GU_PAIRS)
            step_hidden(0)
            last = lambda e: (lambda i: body_q(e, i))
            with dve.Fori(0, E - 1) as e:
                rests(last(e), 0, HT_AFTER)
                hidden_rest(2 * e)
                rests(last(e), HT_AFTER, 12)
                step_hidden(2 * e + 1)
                rows_rest(e + 1)
                rests(last(e), 12, 12 + HT_AFTER)
                hidden_rest(2 * e + 1)
                rests(last(e), 12 + HT_AFTER, 24)
                step_hidden(2 * e + 2)
            rests(last(E - 1), 0, HT_AFTER)
            hidden_rest(2 * E - 2)
            rests(last(E - 1), HT_AFTER, 12)
            step_hidden(2 * E - 1)
            rests(last(E - 1), 12, 16)
            hidden_rest(2 * E - 1)

            dve.wait_ge(grow_in, 16 * 2)
            for c, buf in enumerate((xh, arena)):
                one_over_rms(4 + c)
                for i in range(TILES):
                    normalise(4 + c, buf, buf, i, fin_done)

        @block.tensor
        def _(pe):
            def products(terms):
                for part in range(3):
                    for out, lh, lr, rh, rr, start, stop in terms:
                        lhs, rhs = ((lh, rh), (lh, rr), (lr, rh))[part]
                        done = nc.tensor.matmul(out, lhs, rhs, start=start and part == 0, stop=stop and part == 2)
                return done

            def w(j, lo, n):
                return w_high[:, j, lo:lo + n], w_rest[:, j, lo:lo + n]

            def open_job(b, g, job):
                bank_, before = turn(b, g, job)
                if not (isinstance(before, int) and before == 0):
                    pe.wait_ge(free[bank_], before)
                return bank_

            def pair_ready(n):
                pe.wait_ge(rest_done, n + 1)

            def project_t(b, g, job, n):
                k = open_job(b, g, job)
                if job[1] == "0":
                    pair_ready(n)
                m = int(job[1])
                for kc in range(KC):
                    at = slice(kc * T, (kc + 1) * T)
                    last = products([(bank(k), *w(SLOT["pre" if g is None else stage_name(g)][job[0]], kc * GC + m * P, P),
                                      ut_high[:, at], ut_rest[:, at], kc == 0, kc == KC - 1)])
                last.then_inc(full[k], 1)

            def project_v(b, g, part, n):
                k = open_job(b, g, f"v{part}")
                if part == 0:
                    pair_ready(n)
                for i in (2 * part, 2 * part + 1):
                    for kc in range(KC):
                        at = slice(kc * T + i * P, kc * T + (i + 1) * P)
                        last = products([(bank(k)[:, (i % 2) * GC:(i % 2 + 1) * GC], ut_high[:, at], ut_rest[:, at],
                                          *w(SLOT[stage_name(g)]["v"], kc * GC, GC), kc == 0, kc == KC - 1)])
                last.then_inc(full[k], 1)

            def project_out(b, g, what, lo, hi, n):
                if lo == 0:
                    pair_ready(n)
                for t in range(lo, hi):
                    k = open_job(b, g, f"{what}{t}")
                    i, half = t // 2, t % 2
                    for f in range(2):
                        last = products([(bank(k), ot_high[:, f, i * P:(i + 1) * P], ot_rest[:, f, i * P:(i + 1) * P],
                                          *w(SLOT[stage_name(g)][what], f * D + half * BANK, BANK), f == 0, f == 1)])
                    last.then_inc(full[k], 1)

            def score(A, hh):
                for i in range(TILES):
                    lo = WIN_COL[i] * ROWS
                    last = nc.tensor.matmul(ps[:, 6 * BANK + i * WIN:6 * BANK + (i + 1) * WIN],
                                            qz[:, hh % 2, hh // 2, i * P:(i + 1) * P], kt[:, hh // 2, lo:lo + WIN], start=True, stop=True)
                last.then_inc(s_mm, 1)

            def turn_probabilities(A, hh):
                pe.wait_ge(exp_done, TILES * (A + hh + 1))
                for i in range(TILES):
                    for c in range(2):
                        at = 2 * BANK + i * WIN + c * P
                        last = nc.tensor.transpose(ps[:, at:at + P], scores[:, i, c * P:(c + 1) * P], ident[:, :])
                last.then_inc(pt_mm, 1)

            def values(A, b, g, hh):
                pe.wait_ge(pt_dve, A + hh + 1)
                pe.wait_ge(pt_act, A + hh + 1)
                if not (isinstance(A, int) and A + hh == 0):
                    pe.wait_ge(o_done, A + hh)
                if hh == 0:
                    wait_copied(pe, b, g, "v0")
                    wait_copied(pe, b, g, "v1")
                    pe.wait_ge(voff_in, 32 * (GROUPS * b + g + 1))
                for i in range(TILES):
                    row = WIN_COL[i] * ROWS
                    for c in range(2):
                        vals = (v_off if row % P else v)[:, row // P + c, hh * HD:(hh + 1) * HD]
                        last = nc.tensor.matmul(bank(4)[:, i * HD:(i + 1) * HD], pt[:, i * WIN + c * P:i * WIN + (c + 1) * P],
                                                vals, start=c == 0, stop=c == 1)
                last.then_inc(pv_mm, 1)

            def turn_output(A, b, g):
                pe.wait_ge(o_done, A + GROUP)
                for f in range(2):
                    k = open_job(b, g, f"t{f}")
                    for i in range(TILES):
                        last = nc.tensor.transpose(bank(k)[:, i * P:(i + 1) * P], o[:, i, f * P:(f + 1) * P], ident[:, :])
                    last.then_inc(full[k], 1)

            def group(b, g):
                A = head_count(b, g)
                kind = stage_name(g)
                n = len(PAIRS) * b + SLOTS * g + {"first": 2, "inner": 1, "last": 1}[kind]
                for k in full:
                    pe.wait_ge(free[k], jobs_before(b, g, k))
                score(A, 0)
                project_v(b, g, 0, n)
                turn_probabilities(A, 0)
                score(A, 1)
                project_v(b, g, 1, n)
                if kind == "first":
                    project_t(b, g, "q0", n + 1)
                    values(A, b, g, 0)
                    turn_probabilities(A, 1)
                    score(A, 2)
                    project_t(b, g, "q1", n + 1)
                    values(A, b, g, 1)
                    turn_probabilities(A, 2)
                    score(A, 3)
                    project_t(b, g, "k0", n + 2)
                    values(A, b, g, 2)
                    turn_probabilities(A, 3)
                    project_t(b, g, "k1", n + 2)
                    values(A, b, g, 3)
                    turn_output(A, b, g)
                    return
                cuts = (0, 4, 8) if kind == "inner" else (0, 2, 5, 8)
                project_out(b, g, "w", cuts[0], cuts[1], n + 1)
                values(A, b, g, 0)
                turn_probabilities(A, 1)
                score(A, 2)
                project_out(b, g, "w", cuts[1], cuts[2], n + 1)
                values(A, b, g, 1)
                turn_probabilities(A, 2)
                score(A, 3)
                if kind == "inner":
                    project_t(b, g, "q0", n + 2)
                else:
                    project_out(b, g, "w", cuts[2], cuts[3], n + 1)
                values(A, b, g, 2)
                turn_probabilities(A, 3)
                if kind == "inner":
                    project_t(b, g, "q1", n + 2)
                    values(A, b, g, 3)
                    project_t(b, g, "k0", n + 3)
                    turn_output(A, b, g)
                    project_t(b, g, "k1", n + 3)
                else:
                    values(A, b, g, 3)
                    turn_output(A, b, g)
                    wait_copied(pe, b, g, "t0")
                    wait_copied(pe, b, g, "t1")
                    project_out(b, g, "o", 0, 8, n + 2)

            def turn_x(b):
                pe.wait_ge(xe_done, TILES * (b + 1))
                for kc in range(KC):
                    if kc >= len(NORM_BANKS):
                        pe.wait_ge(utr_done, KC * b + kc - len(NORM_BANKS) + 1)
                    for i in range(TILES):
                        last = nc.tensor.transpose(bank(NORM_BANKS[kc % 4])[:, i * P:(i + 1) * P], early_t[:, i, kc * P:(kc + 1) * P], ident[:, :])
                    last.then_inc(xt_front, 1)
                pe.wait_ge(utr_done, KC * (b + 1))

            def before_groups(b):
                n = len(PAIRS) * b
                for job, pair in (("q0", n), ("q1", n), ("k0", n + 1), ("k1", n + 1)):
                    project_t(b, None, job, pair)

            def router(b):
                pe.wait_ge(xs_done, TILES * (b + 1))

                def chunk(kc):
                    pe.wait_ge(rt_copied, KC * b + kc + 1)
                    for i in range(TILES):
                        last = nc.tensor.matmul(bank(4 + i)[:, 0:E], rt[:, kc % 2, i * P:(i + 1) * P], rw[:, kc, :],
                                                start=kc == 0, stop=kc == KC - 1)
                    last.then_inc(rt_used, 1)

                for kc in range(KC):
                    if kc >= 2:
                        pe.wait_ge(rt_copied, KC * b + kc - 1)
                    for i in range(TILES):
                        last = nc.tensor.transpose(bank(2 + kc % 2)[:, i * P:(i + 1) * P], arena[:, i, kc * P:(kc + 1) * P], ident[:, :])
                    last.then_inc(rt_mm, 1)
                    if kc:
                        chunk(kc - 1)
                chunk(KC - 1)

            pe.wait_ge(const_in, 16 * 3)
            turn_x(0)
            before_groups(0)
            for b in range(TRUNKS):
                pe.wait_ge(zeros_done, 2 * (b + 1))
                if b:
                    pe.wait_ge(lg_step, 2 * b)
                group(b, 0)
                with pe.Fori(1, GROUPS - 1) as g:
                    group(b, g)
                group(b, GROUPS - 1)
                if b + 1 < TRUNKS:
                    turn_x(b + 1)
                    before_groups(b + 1)
                router(b)

            pe.wait_ge(aff_done, 3 * TRUNKS)
            for i in range(TILES):
                last = nc.tensor.transpose(bank(0)[0:TRUNKS * E, i * P:(i + 1) * P], aff[:, i, :], ident[:, :])
            last.then_inc(afft_mm, 1)
            pe.wait_ge(top_done, 4)
            for k, table in enumerate((gv, gi)):
                last = nc.tensor.transpose(bank(1)[:, k * 2 * E:(k + 1) * 2 * E], table[:, :, :].rearrange("e a s -> e (a s)"),
                                           ident[0:TRUNKS * E, 0:TRUNKS * E])
            last.then_inc(route_mm, 1)

            def rows_t(e, before):
                pe.wait_ge(gathered, 16 * (e + 1))
                if before is not None:
                    pe.wait_ge(htr_done, before)
                for kc in range(KC):
                    last = nc.tensor.transpose(bank(6, 2)[:, kc * P:(kc + 1) * P], xg[:, kc * P:(kc + 1) * P], ident[:, :])
                last.then_inc(xt_mm, 1)

            def gate_up(s, q_of):
                for i in range(GU_PAIRS):
                    j = i % SLOTS
                    pe.wait_ge(rest_done, SLOTS * q_of(i) + j + 1)
                    for k in range(2):
                        kc = 2 * (i // 2) + k
                        at = slice(kc * P, (kc + 1) * P)
                        last = products([(bank(2 * (i % 2) + n), xt_high[:, at], xt_rest[:, at], *w(j, k * HALF + n * BANK, BANK),
                                          kc == 0, kc == KC - 1) for n in range(2)])
                    last.then_inc(pair_used, 1)

            def down(s, h, q_of, lo):
                pe.wait_ge(htr_done, s + 1)
                for i in range(lo, lo + D_PAIRS):
                    j = i % SLOTS
                    pe.wait_ge(rest_done, SLOTS * q_of(i) + j + 1)
                    for k in range(2):
                        c = 2 * (i - lo) + k
                        at = slice(c * P, (c + 1) * P)
                        last = products([(bank(4 + n), ht_high[:, at], ht_rest[:, at], *w(j, k * D + n * BANK, BANK),
                                          h == 0 and c == 0, h == 1 and c == 7) for n in range(2)])
                    last.then_inc(pair_used, 1)

            def hidden_t(s):
                pe.wait_ge(hid_done, s + 1)
                for c in range(HALF // P):
                    last = nc.tensor.transpose(bank(6, 2)[:, c * P:(c + 1) * P], hid[:, c * P:(c + 1) * P], ident[:, :])
                last.then_inc(ht_mm, 1)

            rows_t(0, None)
            pe.wait_ge(xtr_done, 1)
            gate_up(0, lambda i: FRONT_Q + i // SLOTS)
            hidden_t(0)
            with pe.Fori(0, E - 1) as e:
                at = lambda s: lambda i: body_q(e, s + i)
                gate_up(2 * e + 1, at(0))
                rows_t(e + 1, 2 * e + 1)
                pe.wait_ge(ys_done, e + 1)
                down(2 * e, 0, at(0), 8)
                pe.wait_ge(xtr_done, e + 2)
                hidden_t(2 * e + 1)
                gate_up(2 * e + 2, at(12))
                down(2 * e + 1, 1, at(0), 20)
                hidden_t(2 * e + 2)
            at = lambda s: lambda i: body_q(E - 1, s + i)
            gate_up(2 * E - 1, at(0))
            pe.wait_ge(ys_done, E)
            down(2 * E - 2, 0, at(0), 8)
            hidden_t(2 * E - 1)
            down(2 * E - 1, 1, at(0), 12)


def bias_layout(rpb):
    q, k = np.arange(P), np.arange(WIN)
    out = []
    for i in (0, 1, 3):
        qc, kcol = QCOLS * i + q // ROWS, WIN_COL[i] + k // ROWS
        start = np.clip(qc - KW // 2, 0, GRID_W - KW)
        inside = (kcol[None] >= start[:, None]) & (kcol[None] < start[:, None] + KW)
        dr = (k % ROWS)[None] - (q % ROWS)[:, None] + KH - 1
        dc = np.where(inside, kcol[None] - qc[:, None] + KW - 1, 0)
        out.append(np.where(inside[None], rpb[:, dr, dc], np.float32(MASKED)))
    return np.ascontiguousarray(np.stack(out, 2).reshape(HEADS * P, 3 * WIN))


def kernel(x_prompt, x_sample, norm_mix_g, norm_ffn_g, final_norm_g, na_w_qkv, na_rpb, na_w_o, pool_w, pool_scale,
           gla_w_in, gla_w_gate_f, gla_b_gate_f, gla_w_gate_b, gla_b_gate_b, gla_norm_g, gla_w_o,
           router_w, moe_w_gate, moe_w_up, moe_w_down):
    import concourse.bacc as bacc
    from concourse.bass_utils import run_bass_kernel_spmd

    by_column = lambda a: np.asarray(a).reshape(ROWS, GRID_W, D).transpose(1, 0, 2).reshape(T, D)
    by_row = lambda a: np.ascontiguousarray(a.reshape(GRID_W, ROWS, D).transpose(1, 0, 2).reshape(1, T, D))
    arrays = {
        "x": np.concatenate([by_column(x_prompt), by_column(x_sample)]),
        "g_mix": np.ascontiguousarray(np.asarray(norm_mix_g).reshape(KC, P).T),
        "g_ffn": np.asarray(norm_ffn_g).reshape(1, D),
        "g_fin": np.asarray(final_norm_g).reshape(1, D),
        "w_qkv": np.asarray(na_w_qkv)[0],
        "bias": bias_layout(np.asarray(na_rpb)[0]),
        "w_o": np.asarray(na_w_o)[0],
        "router_w": np.asarray(router_w)[0],
        "w_gate": np.asarray(moe_w_gate).reshape(E * D, F),
        "w_up": np.asarray(moe_w_up).reshape(E * D, F),
        "w_down": np.asarray(moe_w_down).reshape(E * F, D),
        "identity": np.eye(P, dtype=np.float32),
    }
    nc = bacc.Bacc("TRN2", target_bir_lowering=False, num_devices=1)
    args = {n: nc.dram_tensor(n, a.shape, mybir.dt.from_np(a.dtype), kind="ExternalInput").ap() for n, a in arrays.items()}
    y = nc.dram_tensor("y", (TRUNKS * T, D), F32, kind="ExternalOutput").ap()
    encoder_kernel(nc, *[args[n] for n in arrays], y)
    got = run_bass_kernel_spmd(nc, [arrays], core_ids=[0]).results[0]["y"]
    return by_row(got[:T]), by_row(got[T:])
```

```python
import numpy as np
import concourse.bass as bass
from concourse import mybir
from contextlib import ExitStack

F32 = mybir.dt.float32
F32R = mybir.dt.float32r
U32 = mybir.dt.uint32
ALU = mybir.AluOpType
ACT = mybir.ActivationFunctionType
AX = mybir.AxisListType

P = 128
D = 1024
T = 512
TRUNKS = 2
GRID_W = 64
ROWS = T // GRID_W
KW = 16
KH = 8
HEADS = 16
HD = D // HEADS
E = 16
CAP = 2 * T // E
F = 2048
EPS = 1e-6
MASKED = -1e30

KC = D // P
TILES = T // P
QCOLS = GRID_W // TILES
WIN = 2 * P
WIN_COL = [min(max(QCOLS * i - KW // 2, 0), GRID_W - WIN // ROWS) for i in range(TILES)]
KIND = [0, 1, 1, 2]
GROUP = 4
GROUPS = HEADS // GROUP
GC = GROUP * HD
RAW_SLOTS = 8
SLOTS = 4
PAIR = 2048
HALF = F // 2
BANK = 512
FRONT_Q = TRUNKS * GROUPS
GU_PAIRS = 8
D_PAIRS = 4
OUT_JOBS = [(f"w{n}", b) for n, b in enumerate((0, 1, 5, 0, 1, 5, 0, 1))]
STAGES = {
    "pre": [("q0", 0), ("q1", 1), ("k0", 0), ("k1", 1)],
    "first": [("v0", 5), ("v1", 0), ("q0", 1), ("q1", 5), ("k0", 0), ("k1", 1), ("t0", 5), ("t1", 0)],
    "inner": [("v0", 1), ("v1", 5), *OUT_JOBS, ("q0", 5), ("q1", 0), ("k0", 1), ("t0", 5), ("t1", 0), ("k1", 1)],
    "last": [("v0", 1), ("v1", 5), *OUT_JOBS, ("t0", 5), ("t1", 0),
             *[(f"o{n}", b) for n, b in enumerate((1, 5, 0, 1, 5, 0, 1, 5))]],
}
PAIRS = [("q", 0), ("k", 0), ("v", 0), ("q", 1), ("k", 1), ("v", 1), ("w", 0), ("q", 2), ("k", 2), ("v", 2), ("w", 1),
         ("q", 3), ("k", 3), ("v", 3), ("w", 2), ("w", 3)]
SLOT = {"pre": dict(q=0, k=1), "first": dict(v=2, q=3, k=0), "inner": dict(v=1, w=2, q=3, k=0), "last": dict(v=1, w=2, o=3)}
FRONT_PAIRS = TRUNKS * len(PAIRS)
ADD_BANKS = (0, 2, 6)
ROUTER_BANKS = (2, 6)
NORM_BANKS = (2, 3, 6, 7)
K_BANK = 1


def stage_name(g):
    return {0: "first", GROUPS - 1: "last"}.get(g, "inner") if isinstance(g, int) else "inner"


def jobs_before(b, g, bank):
    pre, first, inner, last = (sum(k == bank for _, k in STAGES[n]) for n in ("pre", "first", "inner", "last"))
    at = b * (pre + first + (GROUPS - 2) * inner + last)
    if g is None:
        return at
    return at + pre + {"first": 0, "inner": first + (g - 1) * inner, "last": first + (GROUPS - 2) * inner}[stage_name(g)]


def turn(b, g, job):
    jobs = STAGES["pre" if g is None else stage_name(g)]
    at = [n for n, _ in jobs].index(job)
    bank = jobs[at][1]
    return bank, jobs_before(b, g, bank) + sum(k == bank for _, k in jobs[:at])


AHEAD = 3
FIN_POOL = (2, 3)
FIN_VECTOR = tuple(t for t in range(TRUNKS * TILES) if t not in FIN_POOL)
HT_AFTER = 6


def encoder_kernel(nc, x, g_mix, g_ffn_col, g_ffn, g_fin, w_qkv, bias, w_o, router_w, w_gate, w_up, w_down, identity, token_numbers, y):
    h_dram = nc.dram_tensor("h_rows", [TRUNKS * T, D], F32).ap()
    u_dram = nc.dram_tensor("u_rows", [TRUNKS * T, D], F32).ap()
    wqkv_v = w_qkv.rearrange("(k p) n -> p k n", p=P)
    wo_v = w_o.rearrange("(k p) n -> p k n", p=P)

    with ExitStack() as ctx:
        def sb(name, shape, dt=F32):
            return ctx.enter_context(nc.sbuf_tensor(name, shape, dt))

        def sem(name):
            return ctx.enter_context(nc.semaphore(name))

        raw = sb("raw", [P, SLOTS, PAIR])
        w_high = sb("w_high", [P, SLOTS, PAIR], F32R)
        w_rest = sb("w_rest", [P, SLOTS, PAIR], F32R)
        xh = sb("xh", [P, TILES, D])
        arena = sb("arena", [P, TILES, D])
        early = sb("early", [P, TILES * D])
        v = sb("v", [P, TILES, GC])
        v_off = sb("v_off", [P, TILES - 1, GC])
        bias_sb = sb("bias_sb", [P, 2, 3, WIN])
        ot_high = sb("ot_high", [P, 2, T], F32R)
        ot_rest = sb("ot_rest", [P, 2, T], F32R)
        grow = sb("grow", [P, D])
        g_col = sb("g_col", [P, KC])
        gf_col = sb("gf_col", [P, KC])
        ident = sb("ident", [P, P])
        rw = sb("rw", [P, KC, E])
        aff = sb("aff", [P, TILES, TRUNKS * E])
        lg = sb("lg", [P, TILES, E])
        ssq = sb("ssq", [P, 24])
        var = sb("var", [P, 24])
        sdev = sb("sdev", [P, 24])
        rstd = sb("rstd", [P, 24])
        newt = sb("newt", [P, 3, 24])
        mx = sb("mx", [P, 2, TILES])
        nmx = sb("nmx", [P, 2, TILES])
        psum_row = sb("psum_row", [P, 2, TILES])
        rinv = sb("rinv", [P, 2, TILES])
        lstat = sb("lstat", [P, TRUNKS, 3, TILES])
        topv = sb("topv", [TRUNKS * E, CAP])
        topi = sb("topi", [TRUNKS * E, CAP], U32)
        topt = sb("topt", [TRUNKS * E, 3, CAP], U32)
        gv = sb("gv", [TRUNKS * E, 2, CAP])
        gi = sb("gi", [TRUNKS * E, 2, CAP])
        gate_w = sb("gate_w", [P, E])
        rows = sb("rows", [P, E], U32)
        last_row = sb("last_row", [P, 1])

        with ExitStack() as front:
            ut_high = front.enter_context(nc.sbuf_tensor("ut_high", [P, KC * T], F32R))
            ut_rest = front.enter_context(nc.sbuf_tensor("ut_rest", [P, KC * T], F32R))
        xt_high, xt_rest = sb("xt_high", [P, D], F32R), sb("xt_rest", [P, D], F32R)
        ht_high, ht_rest = sb("ht_high", [P, D], F32R), sb("ht_rest", [P, D], F32R)
        raw_more = sb("raw_more", [P, 2, PAIR])

        early_t = early[:, :].rearrange("p (i d) -> p i d", i=TILES)
        qz = early[:, 0:4 * T].rearrange("p (a m t) -> p a m t", a=2, m=2)
        kt = early[:, 4 * T:6 * T].rearrange("p (m t) -> p m t", m=2)
        o = early[:, 6 * T:8 * T].rearrange("p (i n) -> p i n", i=TILES)
        scores = arena[:, 3, :].rearrange("p (i k) -> p i k", i=TILES)
        pt = arena[:, 2, :]
        rt = (v[:, :, :].rearrange("p i n -> p (i n)"), arena[:, 1, :])
        squares_junk = arena[:, 3, :]
        affw = v_off[0:TRUNKS * E, 0:2, :].rearrange("e a n -> e (a n)")
        xg = xh[:, 0, :]
        raws = [raw[:, j, :] for j in range(SLOTS)] + [raw_more[:, 0, :], raw_more[:, 1, :],
                                                       early[:, 0:PAIR], early[:, PAIR:2 * PAIR]]
        silu = xh[:, 1, :]
        hid = xh[:, 2, :]
        ys = xh[:, 3, :]
        numbers = v[:, :, :].rearrange("p i n -> p (i n)")
        one_hot = ot_high[:, :, :].rearrange("p f t -> p (f t)")
        ys_high, ys_rest = ht_high, ht_rest
        h_rows = (arena, raw[:, 0:2, :].rearrange("p j (i d) -> p (j i) d", i=2))

        ps = ctx.enter_context(nc.psum_tensor("ps", [P, 8 * BANK], F32))

        def bank(b, n=1):
            return ps[:, b * BANK:(b + n) * BANK]

        const_in = sem("const_in")
        rw_in = sem("rw_in")
        bias_in = [sem(f"bias_in{s}") for s in range(2)]
        xe_in = [[sem(f"xe_in{b}{i}") for i in range(TILES)] for b in range(TRUNKS)]
        xh_in = sem("xh_in")
        grow_in = sem("grow_in")
        full = {k: sem(f"full{k}") for k in (0, 1, 5)}
        free = {k: sem(f"free{k}") for k in (0, 1, 5)}
        raw_in = [sem(f"raw_in{j}") for j in range(RAW_SLOTS)]
        voff_in = sem("voff_in")
        h_out = sem("h_out")
        u_out = sem("u_out")
        gathered = sem("gathered")
        scattered = sem("scattered")
        ys_free = sem("ys_free")
        h_in = [sem(f"h_in{c}") for c in range(TRUNKS)]
        y_out = sem("y_out")
        high_done = sem("high_done")
        rest_done = sem("rest_done")
        pair_used = sem("pair_used")
        zeros_done = sem("zeros_done")
        ssq_xa, ssq_xd = sem("ssq_xa"), sem("ssq_xd")
        ssq_f = sem("ssq_f")
        rstd_x = sem("rstd_x")
        rstd_f = sem("rstd_f")
        ssq_h = sem("ssq_h")
        rstd_done = sem("rstd_done")
        var_done = sem("var_done")
        sdev_done = sem("sdev_done")
        norm_step = sem("norm_step")
        xe_done = sem("xe_done")
        scaled = sem("scaled")
        xs_done = sem("xs_done")
        xt_front = sem("xt_front")
        uth_done = sem("uth_done")
        utr_done = sem("utr_done")
        s_mm = sem("s_mm")
        max_done = sem("max_done")
        nmx_done = sem("nmx_done")
        exp_done = sem("exp_done")
        pt_mm = sem("pt_mm")
        pt_act, pt_dve = sem("pt_act"), sem("pt_dve")
        pv_mm = sem("pv_mm")
        rinv_done = sem("rinv_done")
        o_done = sem("o_done")
        oth_done = sem("oth_done")
        rt_mm = sem("rt_mm")
        rt_act, rt_dve = sem("rt_act"), sem("rt_dve")
        rt_used = sem("rt_used")
        rw_done = sem("rw_done")
        lg_step = sem("lg_step")
        lexp_done = sem("lexp_done")
        aff_done = sem("aff_done")
        afft_mm = sem("afft_mm")
        top_step = sem("top_step")
        top_done = sem("top_done")
        route_mm = sem("route_mm")
        route_done = sem("route_done")
        xt_mm, xth_done, xtr_done = sem("xt_mm"), sem("xth_done"), sem("xtr_done")
        silu_done, hid_done = sem("silu_done"), sem("hid_done")
        ht_mm, hth_done, htr_done = sem("ht_mm"), sem("hth_done"), sem("htr_done")
        numbers_in = sem("numbers_in")
        last_row_done = sem("last_row_done")
        one_hot_done = sem("one_hot_done")
        ysh_done, ysr_done = sem("ysh_done"), sem("ysr_done")
        add_mm = sem("add_mm")
        h_done = sem("h_done")
        fin_scaled = sem("fin_scaled")
        fin_pool = sem("fin_pool")
        ys_done = sem("ys_done")
        fin_done = sem("fin_done")

        block = ctx.enter_context(nc.Block())

        def body_q(e, i):
            return FRONT_Q + GU_PAIRS // SLOTS + (2 * (GU_PAIRS + D_PAIRS) // SLOTS) * e + i // SLOTS

        def body_turn(e, i):
            return GU_PAIRS // RAW_SLOTS + (2 * (GU_PAIRS + D_PAIRS) // RAW_SLOTS) * e + i // RAW_SLOTS

        def pairs_before(e):
            return SLOTS * (body_q(e, 0) - FRONT_Q)

        def wait_full(eng, b, g, job):
            bank, before = turn(b, g, job)
            eng.wait_ge(full[bank], before + 1)
            return bank

        def wait_copied(eng, b, g, job):
            bank, before = turn(b, g, job)
            eng.wait_ge(free[bank], before + 1)

        def head_count(b, g):
            return HEADS * b + GROUP * g

        @block.sync
        def _(sp):

            def load(q, j, src):
                if not (isinstance(q, int) and q == 0):
                    sp.wait_ge(rest_done, SLOTS * (q - 1) + j + 1)
                sp.dma_start(raw[:, j, :].rearrange("p (k n) -> p k n", k=src.shape[1]), src).then_inc(raw_in[j], 16)

            def gate_up_rows(e, h, jj):
                rows_ = (w_gate, w_up)[jj % 2][bass.ds(e * D + (jj // 2) * 2 * P, 2 * P), h * HALF:(h + 1) * HALF]
                return rows_.rearrange("(k p) n -> p k n", p=P)

            def down_rows(e, h, jj):
                return w_down[bass.ds(e * F + h * HALF + jj * 2 * P, 2 * P), :].rearrange("(k p) n -> p k n", p=P)

            def load_pair(e, i, src):
                sp.wait_ge(rest_done, SLOTS * (body_q(e, i) - RAW_SLOTS // SLOTS) + i % SLOTS + 1)
                r = i % RAW_SLOTS
                sp.dma_start(raws[r].rearrange("p (k n) -> p k n", k=src.shape[1]), src).then_inc(raw_in[r], 16)

            def load_first(i):
                if i < SLOTS:
                    return load(FRONT_Q, i, gate_up_rows(0, 0, i))
                if i < SLOTS + 2:
                    sp.wait_ge(voff_in, 32 * TRUNKS * GROUPS)
                elif i == SLOTS + 2:
                    sp.wait_ge(s_mm, HEADS * TRUNKS)
                else:
                    wait_full(sp, TRUNKS - 1, GROUPS - 1, "t1")
                src = gate_up_rows(0, 0, i)
                sp.dma_start(raws[i].rearrange("p (k n) -> p k n", k=src.shape[1]), src).then_inc(raw_in[i], 16)

            def load_nth(n):
                if n >= FRONT_PAIRS:
                    return load_first(n - FRONT_PAIRS)
                what, g = PAIRS[n % len(PAIRS)]
                if what == "w":
                    src = wo_v[:, 2 * g:2 * g + 2, :]
                else:
                    c = "qkv".index(what) * D + g * GC
                    src = wqkv_v[:, :, c:c + GC]
                load(n // SLOTS, n % SLOTS, src)

            def load_bias(A):
                if A >= TRUNKS * HEADS:
                    return
                if A >= 2:
                    sp.wait_ge(max_done, TILES * (A - 1))
                sp.dma_start(bias_sb[:, A % 2, :, :].rearrange("p a k -> p (a k)"),
                             bias[(A % HEADS) * P:(A % HEADS + 1) * P, :]).then_inc(bias_in[A % 2], 16)

            for i in range(TILES):
                sp.dma_start(early_t[:, i, :], x[i * P:(i + 1) * P, :]).then_inc(xe_in[0][i], 16)
            sp.dma_start(ident[:, :], identity).then_inc(const_in, 16)
            sp.dma_start(g_col[:, :], g_mix).then_inc(const_in, 16)
            for n in range(SLOTS):
                load_nth(n)
            sp.dma_start(gf_col[:, :], g_ffn_col).then_inc(rw_in, 16)
            sp.dma_start(rw[:, :, :], router_w.rearrange("(k p) e -> p k e", p=P)).then_inc(rw_in, 16)
            load_bias(0)
            load_bias(1)
            for n in range(SLOTS, 2 * SLOTS):
                load_nth(n)
            for b in range(TRUNKS):
                n = len(PAIRS) * b + 2 * SLOTS
                load_nth(n)
                for g in range(GROUPS):
                    skip = {0: 2, GROUPS - 1: 3}.get(g)
                    for hh in range(GROUP):
                        load_bias(head_count(b, g) + hh + 2)
                        if hh != skip:
                            n += 1
                            load_nth(n)
                n += 1
                load_nth(n)
            def load_run(e, i, rows_of, of, h, count):
                for jj in range(count):
                    load_pair(e, i + jj, rows_of(of, h, jj))

            with sp.Fori(0, E - 1) as e:
                load_run(e, 0, gate_up_rows, e, 1, GU_PAIRS)
                load_run(e, GU_PAIRS, down_rows, e, 0, D_PAIRS)
                load_run(e, GU_PAIRS + D_PAIRS, gate_up_rows, e + 1, 0, GU_PAIRS)
                load_run(e, 2 * GU_PAIRS + D_PAIRS, down_rows, e, 1, D_PAIRS)
            load_run(E - 1, 0, gate_up_rows, E - 1, 1, GU_PAIRS)
            load_run(E - 1, GU_PAIRS, down_rows, E - 1, 0, D_PAIRS)
            load_run(E - 1, GU_PAIRS + D_PAIRS, down_rows, E - 1, 1, D_PAIRS)

            sp.wait_ge(scattered, 16 * (E - 1))
            sp.wait_ge(u_out, 32 * TRUNKS)
            sp.wait_ge(rest_done, SLOTS * body_q(E - 1, RAW_SLOTS + 1) + 2)
            for c in range(TRUNKS):
                sp.dma_start(h_rows[c][:, :, :], h_dram[c * T:(c + 1) * T, :].rearrange("(i p) d -> p i d", p=P)).then_inc(h_in[c], 16)
            for n, t in enumerate(FIN_VECTOR):
                sp.wait_ge(fin_done, n + 1)
                sp.dma_start(y[t * P:(t + 1) * P, :], h_rows[t // TILES][:, t % TILES, :]).then_inc(y_out, 16)
            sp.wait_ge(y_out, 16 * TRUNKS * TILES)

        @block.gpsimd
        def _(pool):
            def load_grow(g):
                pool.dma_start(grow[:, :], g.broadcast_to([P, D])).then_inc(grow_in, 16)

            def rows_of(buf, dram, b, lo=0, hi=TILES):
                return buf[:, lo:hi, :], dram[b * T + lo * P:b * T + hi * P, :].rearrange("(i p) d -> p i d", p=P)

            pool.wait_ge(xe_in[0][TILES - 1], 16)
            pool.dma_start(*rows_of(xh, x, 0)).then_inc(xh_in, 16)
            load_grow(g_ffn)
            for b in range(TRUNKS):
                pool.wait_ge(xt_front, KC * (b + 1))
                nc.gpsimd.memset(qz[HD:P, 0, :, :], 0.0).then_inc(zeros_done, 1)
                nc.gpsimd.memset(qz[0:HD, 1, :, :], 0.0).then_inc(zeros_done, 1)
                if b:
                    pool.wait_ge(u_out, 32 * b)
                    pool.wait_ge(h_out, 16 * b)
                    pool.dma_start(*rows_of(xh, x, b)).then_inc(xh_in, 16)
                if b + 1 < TRUNKS:
                    pool.wait_ge(s_mm, HEADS * (b + 1))
                    for i in range(TILES):
                        if i == TILES - 1:
                            wait_full(pool, b, GROUPS - 1, "t1")
                        pool.dma_start(early_t[:, i, :], x[(b + 1) * T + i * P:(b + 1) * T + (i + 1) * P, :]).then_inc(xe_in[b + 1][i], 16)
                for k in full:
                    pool.wait_ge(free[k], jobs_before(b + 1, None, k))
                out, src = rows_of(xh, h_dram, b)
                pool.dma_start(src, out).then_inc(h_out, 16)
                pool.wait_ge(grow_in, 16)
                for i in range(TILES):
                    pool.wait_ge(scaled, TILES * b + i + 1)
                    nc.gpsimd.tensor_tensor(arena[:, i, :], arena[:, i, :], grow[:, :], ALU.mult).then_inc(xs_done, 1)
                    if i % 2:
                        pool.wait_ge(xs_done, TILES * b + i + 1)
                        out, src = rows_of(arena, u_dram, b, i - 1, i + 1)
                        pool.dma_start(src, out).then_inc(u_out, 16)
            load_grow(g_fin)

            def gather(e):
                pool.indirect_dma_start(xg, None, u_dram, bass.IndirectOffsetOnAxis(ap=rows[:, e:e + 1], axis=0)).then_inc(gathered, 16)

            pool.sem_inc(ys_free, 1)
            pool.wait_ge(u_out, 32 * TRUNKS)
            pool.wait_ge(h_out, 16 * TRUNKS)
            pool.wait_ge(route_done, 1)
            gather(0)
            pool.dma_start(numbers, token_numbers.broadcast_to([P, TRUNKS * T])).then_inc(numbers_in, 16)
            for e in range(E - 1):
                if e + 1 < E:
                    pool.wait_ge(xt_mm, e + 1)
                    gather(e + 1)
                if e:
                    pool.wait_ge(scattered, 16 * e)
                    pool.sem_inc(ys_free, 1)
                pool.wait_ge(ys_done, e + 2)
                pool.indirect_dma_start(h_dram, bass.IndirectOffsetOnAxis(ap=rows[:, e:e + 1], axis=0), ys, None,
                                        compute_op=ALU.add).then_inc(scattered, 16)
            pool.wait_ge(scattered, 16 * (E - 1))
            for n, t in enumerate(FIN_POOL):
                pool.wait_ge(fin_scaled, n + 1)
                row = h_rows[t // TILES][:, t % TILES, :]
                nc.gpsimd.tensor_tensor(row, row, grow[:, :], ALU.mult).then_inc(fin_pool, 1)

        @block.scalar
        def _(act):
            def high(q, j):
                act.wait_ge(raw_in[j], 16 * (q + 1))
                nc.scalar.copy(w_high[:, j, :], raw[:, j, :]).then_inc(high_done, 1)

            def square(c, src, i, junk, done):
                nc.scalar.activation(junk, src[:, i, :], ACT.Square, accum_out=ssq[:, TILES * c + i:TILES * c + i + 1]).then_inc(done, 1)

            def root(c):
                act.wait_ge(var_done, c + 1)
                nc.scalar.activation(sdev[:, TILES * c:TILES * (c + 1)], var[:, TILES * c:TILES * (c + 1)], ACT.Sqrt).then_inc(sdev_done, 1)

            def exponentials(A, hh):
                act.wait_ge(nmx_done, A + hh + 1)
                for i in range(TILES):
                    nc.scalar.activation(scores[:, i, :], scores[:, i, :], ACT.Exp, bias=nmx[:, hh % 2, i:i + 1],
                                         accum_out=psum_row[:, hh % 2, i:i + 1]).then_inc(exp_done, 1)

            def copy_pt(A, hh):
                act.wait_ge(pt_mm, A + hh + 1)
                nc.scalar.copy(pt[:, 512:1024], bank(3)).then_inc(pt_act, 1)

            def copy_v(b, g, part):
                k = wait_full(act, b, g, f"v{part}")
                nc.scalar.copy(v[:, 2 * part:2 * part + 2, :].rearrange("p i n -> p (i n)"), bank(k)).then_inc(free[k], 1)

            def shift_v(b, g):
                wait_copied(act, b, g, "v0")
                wait_copied(act, b, g, "v1")
                act.dma_start(v_off[0:HD, :, :], v[HD:P, 0:TILES - 1, :]).then_inc(voff_in, 16)
                act.dma_start(v_off[HD:P, :, :], v[0:HD, 1:TILES, :]).then_inc(voff_in, 16)

            def copy_q(b, g, m):
                k = wait_full(act, b, g, f"q{m}")
                nc.scalar.mul(qz[0:HD, 0, m, :], bank(k)[0:HD, :], HD ** -0.5)
                nc.scalar.mul(qz[HD:P, 1, m, :], bank(k)[HD:P, :], HD ** -0.5).then_inc(free[k], 1)

            def split_ot(b, g):
                for f in range(2):
                    k = wait_full(act, b, g, f"t{f}")
                    nc.scalar.copy(ot_high[:, f, :], bank(k)).then_inc(oth_done, 1)

            def next_high(b, g, what, last_job, q):
                wait_full(act, b, g, last_job)
                high(q, SLOT["pre" if g is None else stage_name(g)][what])

            def x_squares(b, i):
                act.wait_ge(xe_in[b][i], 16)
                if i:
                    act.wait_ge(ssq_xa, 2 * b + 1)
                square(b, early_t, i, arena[:, 0, :], ssq_xa)

            def split_x(b):
                for kc in range(KC):
                    act.wait_ge(xt_front, KC * b + kc + 1)
                    nc.scalar.activation(ut_high[:, kc * T:(kc + 1) * T], bank(NORM_BANKS[kc % 4]), ACT.Copy,
                                         scale=g_col[:, kc:kc + 1]).then_inc(uth_done, 1)

            def before_groups(b):
                copy_q(b, None, 0)
                copy_q(b, None, 1)
                next_high(b, None, "q", "q1", SLOTS * b + 1)

            def h_squares(b, i):
                wait_copied(act, b, GROUPS - 1, f"o{2 * i}")
                wait_copied(act, b, GROUPS - 1, f"o{2 * i + 1}")
                if i:
                    act.wait_ge(ssq_h, TILES * b + i)
                square(TRUNKS + b, xh, i, squares_junk, ssq_h)

            def copy_h(b, i):
                act.wait_ge(rt_mm, TILES * b + i + 1)
                nc.scalar.copy(rt[i % 2][:, 0:BANK], bank(ROUTER_BANKS[i % 2])).then_inc(rt_act, 1)

            def scale_h(b):
                act.wait_ge(rstd_done, b + 1)
                act.wait_ge(rt_used, TILES * (b + 1))
                for i in range(TILES):
                    at = TILES * (TRUNKS + b) + i
                    nc.scalar.activation(arena[:, i, :], xh[:, i, :], ACT.Copy, scale=rstd[:, at:at + 1]).then_inc(scaled, 1)

            def exp_logits(b):
                act.wait_ge(lg_step, 3 * (b + 1))
                nc.scalar.activation(lg[:, :, :], lg[:, :, :], ACT.Exp).then_inc(lexp_done, 1)

            def group(b, g):
                A = head_count(b, g)
                kind = stage_name(g)
                at = SLOTS * b + g + 1
                exponentials(A, 0)
                act.wait_ge(full[K_BANK], jobs_before(b, g, K_BANK))
                high(at, 1 if kind == "first" else 0)
                copy_v(b, g, 0)
                copy_pt(A, 0)
                exponentials(A, 1)
                copy_v(b, g, 1)
                shift_v(b, g)
                next_high(b, g, "v", "v1", at)
                copy_pt(A, 1)
                exponentials(A, 2)
                if kind != "first":
                    next_high(b, g, "w", "w7", at)
                copy_pt(A, 2)
                exponentials(A, 3)
                if kind == "last":
                    copy_pt(A, 3)
                else:
                    copy_q(b, g, 0)
                    if kind == "inner":
                        copy_pt(A, 3)
                    copy_q(b, g, 1)
                    next_high(b, g, "q", "q1", at)
                    if kind == "first":
                        copy_pt(A, 3)
                split_ot(b, g)

            act.sem_inc(ys_done, 1)
            for i in (0, 2):
                x_squares(0, i)
            root(0)
            high(0, 0)
            act.wait_ge(const_in, 16 * 2)
            split_x(0)
            for j in range(1, SLOTS):
                high(0, j)
            before_groups(0)
            for b in range(TRUNKS):
                group(b, 0)
                with act.Fori(1, GROUPS - 1) as g:
                    group(b, g)
                group(b, GROUPS - 1)
                if b + 1 < TRUNKS:
                    x_squares(b + 1, 0)
                    x_squares(b + 1, 2)
                for i in range(TILES - 1):
                    h_squares(b, i)
                    copy_h(b, i)
                if b + 1 < TRUNKS:
                    root(b + 1)
                h_squares(b, TILES - 1)
                copy_h(b, TILES - 1)
                root(TRUNKS + b)
                if b + 1 == TRUNKS:
                    exp_logits(b)
                    scale_h(b)
                next_high(b, GROUPS - 1, "o", "o7", SLOTS * (b + 1))
                if b + 1 < TRUNKS:
                    split_x(b + 1)
                    exp_logits(b)
                    scale_h(b)
                    before_groups(b + 1)

            def step_silu(s, used_by_gate_up):
                act.wait_ge(pair_used, used_by_gate_up)
                nc.scalar.activation(silu, bank(0, 2), ACT.Silu).then_inc(silu_done, 1)

            def rows_high(e):
                act.wait_ge(xt_mm, e + 1)
                nc.scalar.copy(xt_high[:, :], bank(6, 2)).then_inc(xth_done, 1)

            def hidden_high(s):
                act.wait_ge(ht_mm, s + 1)
                nc.scalar.copy(ht_high[:, :], bank(6, 2)).then_inc(hth_done, 1)

            def result(e, used_by_down):
                act.wait_ge(pair_used, used_by_down)
                act.wait_ge(ys_free, e + 1)
                nc.scalar.activation(ys, bank(4, 2), ACT.Copy, scale=gate_w[:, bass.ds(e, 1)]).then_inc(ys_done, 1)

            def highs(e, lo, hi):
                for i in range(lo, hi):
                    q, before = (FRONT_Q + i // SLOTS, 0) if e is None else (body_q(e, i), body_turn(e, i))
                    act.wait_ge(pair_used, SLOTS * (q - FRONT_Q - 1) + i % SLOTS + 1)
                    act.wait_ge(raw_in[i % RAW_SLOTS], 16 * ((FRONT_Q if i % RAW_SLOTS < SLOTS else 0) + before + 1))
                    nc.scalar.copy(w_high[:, i % SLOTS, :], raws[i % RAW_SLOTS]).then_inc(high_done, 1)

            rows_high(0)
            highs(None, SLOTS, GU_PAIRS)
            highs(0, 0, AHEAD)
            step_silu(0, GU_PAIRS)
            highs(0, AHEAD, HT_AFTER)
            hidden_high(0)
            with act.Fori(0, E - 1) as e:
                highs(e, HT_AFTER, 12)
                step_silu(2 * e + 1, pairs_before(e) + GU_PAIRS)
                rows_high(e + 1)
                highs(e, 12, 12 + HT_AFTER)
                hidden_high(2 * e + 1)
                highs(e, 12 + HT_AFTER, 24)
                step_silu(2 * e + 2, pairs_before(e) + 2 * GU_PAIRS + D_PAIRS)
                highs(e + 1, 0, HT_AFTER)
                hidden_high(2 * e + 2)
                result(e, pairs_before(e) + 2 * (GU_PAIRS + D_PAIRS))
            highs(E - 1, HT_AFTER, 12)
            step_silu(2 * E - 1, pairs_before(E - 1) + GU_PAIRS)
            highs(E - 1, 12, 14)
            act.wait_ge(ht_mm, 2 * E)
            nc.scalar.copy(xt_high[:, :], bank(6, 2)).then_inc(hth_done, 1)
            highs(E - 1, 14, 16)
            act.wait_ge(pair_used, pairs_before(E - 1) + GU_PAIRS + 2 * D_PAIRS)
            nc.scalar.activation(ys_high[:, :], bank(4, 2), ACT.Copy, scale=gate_w[:, E - 1:E]).then_inc(ysh_done, 1)

            for c in range(TRUNKS):
                for i in range(TILES):
                    t = TILES * c + i
                    act.wait_ge(h_done, t + 1)
                    if t >= 2:
                        act.wait_ge(ssq_f, t - 1)
                    square(4 + c, h_rows[c], i, xh[:, t % 2, :], ssq_f)
                root(4 + c)
            for n, t in enumerate(FIN_POOL):
                c, i = t // TILES, t % TILES
                act.wait_ge(rstd_f, c + 1)
                nc.scalar.activation(h_rows[c][:, i, :], h_rows[c][:, i, :], ACT.Copy,
                                     scale=rstd[:, TILES * (4 + c) + i:TILES * (4 + c) + i + 1]).then_inc(fin_scaled, 1)
            for n, t in enumerate(FIN_POOL):
                act.wait_ge(fin_pool, n + 1)
                act.dma_start(y[t * P:(t + 1) * P, :], h_rows[t // TILES][:, t % TILES, :]).then_inc(y_out, 16)

        @block.vector
        def _(dve):
            def rest(q, j, r=None):
                dve.wait_ge(high_done, SLOTS * q + j + 1)
                nc.vector.tensor_tensor(w_rest[:, j, :], raws[j if r is None else r], w_high[:, j, :].bitcast(F32), ALU.subtract).then_inc(rest_done, 1)

            def one_over_rms(c):
                cols = slice(TILES * c, TILES * (c + 1))
                if c < TRUNKS:
                    dve.wait_ge(ssq_xa, 2 * (c + 1))
                    dve.wait_ge(ssq_xd, 2 * (c + 1))
                else:
                    dve.wait_ge(ssq_h if c < 2 * TRUNKS else ssq_f, TILES * (c % TRUNKS + 1))
                nc.vector.tensor_scalar(var[:, cols], ssq[:, cols], 1.0 / D, EPS, ALU.mult, ALU.add).then_inc(var_done, 1)
                dve.wait_ge(sdev_done, c + 1)
                n = 4 * c

                nc.vector.reciprocal(newt[:, 0, cols], sdev[:, cols]).then_inc(norm_step, 1)
                dve.wait_ge(norm_step, n + 1)
                nc.vector.tensor_tensor(newt[:, 1, cols], newt[:, 0, cols], newt[:, 0, cols], ALU.mult).then_inc(norm_step, 1)
                dve.wait_ge(norm_step, n + 2)
                nc.vector.tensor_tensor(newt[:, 2, cols], newt[:, 1, cols], var[:, cols], ALU.mult).then_inc(norm_step, 1)
                dve.wait_ge(norm_step, n + 3)
                nc.vector.tensor_scalar(newt[:, 1, cols], newt[:, 2, cols], -0.5, 1.5, ALU.mult, ALU.add).then_inc(norm_step, 1)
                dve.wait_ge(norm_step, n + 4)
                done = (rstd_x, rstd_done, rstd_f)[c // TRUNKS]
                nc.vector.tensor_tensor(rstd[:, cols], newt[:, 0, cols], newt[:, 1, cols], ALU.mult).then_inc(done, 1)
                dve.wait_ge(done, c % TRUNKS + 1)

            def normalise(c, dst, src, i, done):
                nc.vector.scalar_tensor_tensor(out=dst[:, i, :], in0=src[:, i, :], scalar=rstd[:, TILES * c + i:TILES * c + i + 1],
                                               in1=grow[:, :], op0=ALU.mult, op1=ALU.mult).then_inc(done, 1)

            def biased(A, b, g, hh):
                dve.wait_ge(s_mm, A + hh + 1)
                dve.wait_ge(bias_in[hh % 2], 16 * (HEADS // 2 * b + GROUP // 2 * g + hh // 2 + 1))
                nc.vector.memset(nmx[:, hh % 2, :], 0.0)
                for i in range(TILES):
                    nc.vector.tensor_tensor_reduce(out=scores[:, i, :], in0=ps[:, 6 * BANK + i * WIN:6 * BANK + (i + 1) * WIN],
                                                   in1=bias_sb[:, hh % 2, KIND[i], :], scale=1.0, scalar=-3e38, op0=ALU.add,
                                                   op1=ALU.max, accum_out=mx[:, hh % 2, i:i + 1]).then_inc(max_done, 1)
                dve.wait_ge(max_done, TILES * (A + hh + 1))
                nc.vector.tensor_scalar(nmx[:, hh % 2, :], mx[:, hh % 2, :], -1.0, None, ALU.mult).then_inc(nmx_done, 1)

            def copy_pt(A, hh):
                dve.wait_ge(pt_mm, A + hh + 1)
                nc.vector.tensor_copy(pt[:, 0:512], bank(2)).then_inc(pt_dve, 1)

            def output(A, hh):
                s = hh % 2
                nc.vector.reciprocal(rinv[:, s, :], psum_row[:, s, :]).then_inc(rinv_done, 1)
                dve.wait_ge(rinv_done, A + hh + 1)
                dve.wait_ge(pv_mm, A + hh + 1)
                nc.vector.tensor_tensor(o[:, :, hh * HD:(hh + 1) * HD],
                                        bank(4)[:, 0:TILES * HD].rearrange("p (i n) -> p i n", i=TILES),
                                        rinv[:, s, :].rearrange("p (i a) -> p i a", a=1).broadcast_to([P, TILES, HD]), ALU.mult).then_inc(o_done, 1)

            def copy_k(b, g, m):
                k = wait_full(dve, b, g, f"k{m}")
                nc.vector.tensor_copy(kt[:, m, :], bank(k)).then_inc(free[k], 1)

            def split_ot(b, g):
                for f in range(2):
                    k, _ = turn(b, g, f"t{f}")
                    dve.wait_ge(oth_done, 2 * (GROUPS * b + g) + f + 1)
                    nc.vector.tensor_tensor(ot_rest[:, f, :], bank(k), ot_high[:, f, :].bitcast(F32), ALU.subtract).then_inc(free[k], 1)

            def add_out(b, g, what, lo, hi):
                for n in range(lo, hi):
                    k = wait_full(dve, b, g, f"{what}{n}")
                    part = xh[:, n // 2, (n % 2) * BANK:(n % 2 + 1) * BANK]
                    nc.vector.tensor_tensor(part, bank(k), part, ALU.add).then_inc(free[k], 1)

            def x_squares(b, i):
                dve.wait_ge(xe_in[b][i], 16)
                if i > 1:
                    dve.wait_ge(ssq_xd, 2 * b + 1)
                at = TILES * b + i
                nc.vector.tensor_tensor_reduce(out=arena[:, 2, :], in0=early_t[:, i, :], in1=early_t[:, i, :], scale=1.0,
                                               scalar=0.0, op0=ALU.mult, op1=ALU.add, accum_out=ssq[:, at:at + 1]).then_inc(ssq_xd, 1)

            def x_scale(b):
                for i in range(TILES):
                    nc.vector.tensor_scalar(early_t[:, i, :], early_t[:, i, :], rstd[:, TILES * b + i:TILES * b + i + 1], None,
                                            ALU.mult).then_inc(xe_done, 1)

            def copy_h(b, i):
                dve.wait_ge(rt_mm, TILES * b + i + 1)
                nc.vector.tensor_copy(rt[i % 2][:, BANK:2 * BANK], bank(ROUTER_BANKS[i % 2] + 1)).then_inc(rt_dve, 1)

            def split_x(b):
                for kc in range(KC):
                    dve.wait_ge(uth_done, KC * b + kc + 1)
                    nc.vector.scalar_tensor_tensor(out=ut_rest[:, kc * T:(kc + 1) * T], in0=bank(NORM_BANKS[kc % 4]),
                                                   scalar=g_col[:, kc:kc + 1], in1=ut_high[:, kc * T:(kc + 1) * T].bitcast(F32),
                                                   op0=ALU.mult, op1=ALU.subtract).then_inc(utr_done, 1)

            def before_groups(b):
                rest(SLOTS * b + 1, 0)
                copy_k(b, None, 0)
                copy_k(b, None, 1)

            def group(b, g):
                A = head_count(b, g)
                kind = stage_name(g)
                at = SLOTS * b + g + 1
                biased(A, b, g, 0)
                rest(at, 1 if kind == "first" else 0)
                copy_pt(A, 0)
                biased(A, b, g, 1)
                if kind == "first":
                    output(A, 0)
                    copy_pt(A, 1)
                    biased(A, b, g, 2)
                    rest(at, SLOT[kind]["v"])
                    output(A, 1)
                    copy_pt(A, 2)
                    biased(A, b, g, 3)
                    rest(at, SLOT[kind]["q"])
                    copy_k(b, g, 0)
                    output(A, 2)
                    copy_pt(A, 3)
                    copy_k(b, g, 1)
                    output(A, 3)
                    split_ot(b, g)
                    return
                cuts = (0, 4, 8, 8) if kind == "inner" else (0, 2, 5, 8)
                add_out(b, g, "w", cuts[0], cuts[1])
                output(A, 0)
                copy_pt(A, 1)
                biased(A, b, g, 2)
                rest(at, SLOT[kind]["v"])
                add_out(b, g, "w", cuts[1], cuts[2])
                if kind == "inner":
                    rest(at, SLOT[kind]["w"])
                output(A, 1)
                copy_pt(A, 2)
                biased(A, b, g, 3)
                if kind == "last":
                    add_out(b, g, "w", cuts[2], cuts[3])
                    rest(at, SLOT[kind]["w"])
                output(A, 2)
                copy_pt(A, 3)
                if kind == "inner":
                    output(A, 3)
                    copy_k(b, g, 0)
                    split_ot(b, g)
                    rest(at, SLOT[kind]["q"])
                    copy_k(b, g, 1)
                else:
                    output(A, 3)
                    split_ot(b, g)
                    add_out(b, g, "o", 0, 3)
                    copy_h(b, 0)
                    add_out(b, g, "o", 3, 5)
                    copy_h(b, 1)
                    if b + 1 < TRUNKS:
                        x_squares(b + 1, 1)
                    add_out(b, g, "o", 5, 7)
                    copy_h(b, 2)
                    add_out(b, g, "o", 7, 8)
                    if b + 1 < TRUNKS:
                        x_squares(b + 1, 3)

            for i in (1, 3):
                x_squares(0, i)
            one_over_rms(0)
            x_scale(0)
            rest(0, 0)
            split_x(0)
            dve.wait_ge(rw_in, 16 * 2)
            nc.vector.tensor_tensor(rw[:, :, :], rw[:, :, :], gf_col[:, :].rearrange("p (k a) -> p k a", a=1).broadcast_to([P, KC, E]),
                                    ALU.mult).then_inc(rw_done, 1)
            for j in range(1, SLOTS):
                rest(0, j)
            before_groups(0)
            for b in range(TRUNKS):
                dve.wait_ge(xh_in, 16 * (b + 1))
                if b:
                    dve.wait_ge(u_out, 32 * b)
                group(b, 0)
                with dve.Fori(1, GROUPS - 1) as g:
                    group(b, g)
                group(b, GROUPS - 1)
                if b + 1 < TRUNKS:
                    one_over_rms(b + 1)
                copy_h(b, TILES - 1)
                one_over_rms(TRUNKS + b)
                if b + 1 < TRUNKS:
                    x_scale(b + 1)
                    rest(SLOTS * (b + 1), SLOT["last"]["o"])
                    split_x(b + 1)

                logits = bank(4)[:, 0:TILES * E].rearrange("p (i n) -> p i n", i=TILES)
                spread = lambda a: a.rearrange("p (i a) -> p i a", a=1).broadcast_to([P, TILES, E])
                dve.wait_ge(rt_used, TILES * (b + 1))
                nc.vector.tensor_tensor(lg[:, :, :], logits, spread(rstd[:, TILES * (TRUNKS + b):TILES * (TRUNKS + b + 1)]), ALU.mult).then_inc(lg_step, 1)
                dve.wait_ge(lg_step, 3 * b + 1)
                nc.vector.tensor_reduce(lstat[:, b, 0, :], lg[:, :, :], AX.X, ALU.max).then_inc(lg_step, 1)
                dve.wait_ge(lg_step, 3 * b + 2)
                nc.vector.tensor_tensor(lg[:, :, :], lg[:, :, :], spread(lstat[:, b, 0, :]), ALU.subtract).then_inc(lg_step, 1)
                dve.wait_ge(lexp_done, b + 1)
                nc.vector.tensor_reduce(lstat[:, b, 1, :], lg[:, :, :], AX.X, ALU.add).then_inc(aff_done, 1)
                dve.wait_ge(aff_done, 3 * b + 1)
                nc.vector.reciprocal(lstat[:, b, 2, :], lstat[:, b, 1, :]).then_inc(aff_done, 1)
                dve.wait_ge(aff_done, 3 * b + 2)
                nc.vector.tensor_tensor(aff[:, :, b * E:(b + 1) * E], lg[:, :, :], spread(lstat[:, b, 2, :]), ALU.mult).then_inc(aff_done, 1)
                dve.wait_ge(aff_done, 3 * b + 3)
                if b + 1 < TRUNKS:
                    before_groups(b + 1)

            count = 0

            def link(instruction):
                nonlocal count
                count += 1
                instruction.then_inc(top_step, 1)
                dve.wait_ge(top_step, count)

            dve.wait_ge(afft_mm, 1)
            link(nc.vector.tensor_copy(affw.rearrange("e (r i c) -> e r i c", r=ROWS, i=TILES),
                                       bank(0)[0:TRUNKS * E, :].rearrange("e (i c r) -> e r i c", i=TILES, r=ROWS)))
            for k in range(CAP // 8):
                best = topv[:, 8 * k:8 * k + 8]
                link(nc.vector.max(best, affw))
                link(nc.vector.max_index(topi[:, 8 * k:8 * k + 8], best, affw))
                if k + 1 < CAP // 8:
                    link(nc.vector.match_replace(affw, best, affw, -1.0))
            link(nc.vector.tensor_scalar(topt[:, 0, :], topi[:, :], GRID_W - 1, ROWS.bit_length() - 1, ALU.bitwise_and, ALU.logical_shift_left))
            link(nc.vector.tensor_scalar(topt[:, 1, :], topi[:, :], GRID_W.bit_length() - 1, None, ALU.logical_shift_right))
            link(nc.vector.tensor_tensor(topt[:, 2, :], topt[:, 0, :], topt[:, 1, :], ALU.bitwise_or))
            for k in range(2):
                nc.vector.tensor_copy(gv[:, k, :], topv[:, :]).then_inc(top_done, 1)
                nc.vector.tensor_copy(gi[:, k, :], topt[:, 2, :]).then_inc(top_done, 1)
            dve.wait_ge(route_mm, 1)
            link(nc.vector.tensor_copy(gate_w[0:CAP, :], bank(1)[0:CAP, 0:E]))
            link(nc.vector.tensor_copy(gate_w[CAP:P, :], bank(1)[CAP:P, E:2 * E]))
            link(nc.vector.tensor_copy(rows[0:CAP, :], bank(1)[0:CAP, 2 * E:3 * E]))
            nc.vector.tensor_scalar(rows[CAP:P, :], bank(1)[CAP:P, 3 * E:4 * E], float(T), None, ALU.add).then_inc(route_done, 1)

            def step_hidden(s):
                dve.wait_ge(silu_done, s + 1)
                nc.vector.tensor_tensor(hid, bank(2, 2), silu, ALU.mult).then_inc(hid_done, 1)

            def rows_rest(e):
                dve.wait_ge(xth_done, e + 1)
                nc.vector.tensor_tensor(xt_rest[:, :], bank(6, 2), xt_high[:, :].bitcast(F32), ALU.subtract).then_inc(xtr_done, 1)

            def hidden_rest(s):
                dve.wait_ge(hth_done, s + 1)
                nc.vector.tensor_tensor(ht_rest[:, :], bank(6, 2), ht_high[:, :].bitcast(F32), ALU.subtract).then_inc(htr_done, 1)

            def rests(e, lo, hi):
                for i in range(lo, hi):
                    rest(FRONT_Q + i // SLOTS if e is None else body_q(e, i), i % SLOTS, i % RAW_SLOTS)

            rest(FRONT_Q, SLOT["last"]["o"])
            rows_rest(0)
            rests(None, SLOTS, GU_PAIRS)
            rests(0, 0, AHEAD)
            step_hidden(0)
            with dve.Fori(0, E - 1) as e:
                rests(e, AHEAD, HT_AFTER)
                hidden_rest(2 * e)
                rests(e, HT_AFTER, 12)
                step_hidden(2 * e + 1)
                rows_rest(e + 1)
                rests(e, 12, 12 + HT_AFTER)
                hidden_rest(2 * e + 1)
                rests(e, 12 + HT_AFTER, 24)
                step_hidden(2 * e + 2)
                rests(e + 1, 0, AHEAD)
            rests(E - 1, AHEAD, HT_AFTER)
            hidden_rest(2 * E - 2)
            rests(E - 1, HT_AFTER, 12)
            step_hidden(2 * E - 1)
            rests(E - 1, 12, 14)
            dve.wait_ge(hth_done, 2 * E)
            nc.vector.tensor_tensor(xt_rest[:, :], bank(6, 2), xt_high[:, :].bitcast(F32), ALU.subtract).then_inc(htr_done, 1)
            rests(E - 1, 14, 16)
            dve.wait_ge(numbers_in, 16)
            nc.vector.tensor_copy(last_row[:, :], rows[:, E - 1:E]).then_inc(last_row_done, 1)
            dve.wait_ge(last_row_done, 1)
            nc.vector.tensor_scalar(one_hot, numbers, last_row[:, 0:1], None, ALU.is_equal).then_inc(one_hot_done, 1)
            dve.wait_ge(ysh_done, 1)
            nc.vector.scalar_tensor_tensor(out=ys_rest[:, :], in0=bank(4, 2), scalar=gate_w[:, E - 1:E], in1=ys_high[:, :].bitcast(F32),
                                           op0=ALU.mult, op1=ALU.subtract).then_inc(ysr_done, 1)

            for t in range(TRUNKS * TILES):
                row = h_rows[t // TILES][:, t % TILES, :]
                if t % TILES == 0:
                    dve.wait_ge(h_in[t // TILES], 16)
                dve.wait_ge(add_mm, t + 1)
                nc.vector.tensor_tensor(row, bank(ADD_BANKS[t % 3], 2), row, ALU.add).then_inc(h_done, 1)
            dve.wait_ge(grow_in, 16 * 2)
            for c in range(TRUNKS):
                one_over_rms(4 + c)
                for i in range(TILES):
                    if TILES * c + i in FIN_VECTOR:
                        normalise(4 + c, h_rows[c], h_rows[c], i, fin_done)

        @block.tensor
        def _(pe):
            def products(terms):
                for part in range(3):
                    for out, lh, lr, rh, rr, start, stop in terms:
                        lhs, rhs = ((lh, rh), (lh, rr), (lr, rh))[part]
                        done = nc.tensor.matmul(out, lhs, rhs, start=start and part == 0, stop=stop and part == 2)
                return done

            def w(j, lo, n):
                return w_high[:, j, lo:lo + n], w_rest[:, j, lo:lo + n]

            def open_job(b, g, job):
                bank_, before = turn(b, g, job)
                if not (isinstance(before, int) and before == 0):
                    pe.wait_ge(free[bank_], before)
                return bank_

            def pair_ready(n):
                pe.wait_ge(rest_done, n + 1)

            def project_t(b, g, job, n):
                k = open_job(b, g, job)
                if job[1] == "0":
                    pair_ready(n)
                m = int(job[1])
                for kc in range(KC):
                    if g is None and job == "q0":
                        pe.wait_ge(utr_done, KC * b + kc + 1)
                    at = slice(kc * T, (kc + 1) * T)
                    last = products([(bank(k), *w(SLOT["pre" if g is None else stage_name(g)][job[0]], kc * GC + m * P, P),
                                      ut_high[:, at], ut_rest[:, at], kc == 0, kc == KC - 1)])
                last.then_inc(full[k], 1)

            def project_v(b, g, part, n):
                k = open_job(b, g, f"v{part}")
                if part == 0:
                    pair_ready(n)
                for i in (2 * part, 2 * part + 1):
                    for kc in range(KC):
                        at = slice(kc * T + i * P, kc * T + (i + 1) * P)
                        last = products([(bank(k)[:, (i % 2) * GC:(i % 2 + 1) * GC], ut_high[:, at], ut_rest[:, at],
                                          *w(SLOT[stage_name(g)]["v"], kc * GC, GC), kc == 0, kc == KC - 1)])
                last.then_inc(full[k], 1)

            def project_out(b, g, what, lo, hi, n):
                if lo == 0:
                    pair_ready(n)
                for t in range(lo, hi):
                    k = open_job(b, g, f"{what}{t}")
                    i, half = t // 2, t % 2
                    for f in range(2):
                        last = products([(bank(k), ot_high[:, f, i * P:(i + 1) * P], ot_rest[:, f, i * P:(i + 1) * P],
                                          *w(SLOT[stage_name(g)][what], f * D + half * BANK, BANK), f == 0, f == 1)])
                    last.then_inc(full[k], 1)

            def score(A, hh):
                for i in range(TILES):
                    lo = WIN_COL[i] * ROWS
                    last = nc.tensor.matmul(ps[:, 6 * BANK + i * WIN:6 * BANK + (i + 1) * WIN],
                                            qz[:, hh % 2, hh // 2, i * P:(i + 1) * P], kt[:, hh // 2, lo:lo + WIN], start=True, stop=True)
                last.then_inc(s_mm, 1)

            def turn_probabilities(A, hh):
                pe.wait_ge(exp_done, TILES * (A + hh + 1))
                for i in range(TILES):
                    for c in range(2):
                        at = 2 * BANK + i * WIN + c * P
                        last = nc.tensor.transpose(ps[:, at:at + P], scores[:, i, c * P:(c + 1) * P], ident[:, :])
                last.then_inc(pt_mm, 1)

            def values(A, b, g, hh):
                pe.wait_ge(pt_dve, A + hh + 1)
                pe.wait_ge(pt_act, A + hh + 1)
                if not (isinstance(A, int) and A + hh == 0):
                    pe.wait_ge(o_done, A + hh)
                if hh == 0:
                    wait_copied(pe, b, g, "v0")
                    wait_copied(pe, b, g, "v1")
                    pe.wait_ge(voff_in, 32 * (GROUPS * b + g + 1))
                for i in range(TILES):
                    row = WIN_COL[i] * ROWS
                    for c in range(2):
                        vals = (v_off if row % P else v)[:, row // P + c, hh * HD:(hh + 1) * HD]
                        last = nc.tensor.matmul(bank(4)[:, i * HD:(i + 1) * HD], pt[:, i * WIN + c * P:i * WIN + (c + 1) * P],
                                                vals, start=c == 0, stop=c == 1)
                last.then_inc(pv_mm, 1)

            def turn_output(A, b, g):
                pe.wait_ge(o_done, A + GROUP)
                for f in range(2):
                    k = open_job(b, g, f"t{f}")
                    for i in range(TILES):
                        last = nc.tensor.transpose(bank(k)[:, i * P:(i + 1) * P], o[:, i, f * P:(f + 1) * P], ident[:, :])
                    last.then_inc(full[k], 1)

            def group(b, g):
                A = head_count(b, g)
                kind = stage_name(g)
                n = len(PAIRS) * b + SLOTS * g + {"first": 2, "inner": 1, "last": 1}[kind]
                for k in full:
                    pe.wait_ge(free[k], jobs_before(b, g, k))
                score(A, 0)
                project_v(b, g, 0, n)
                turn_probabilities(A, 0)
                score(A, 1)
                project_v(b, g, 1, n)
                if kind == "first":
                    project_t(b, g, "q0", n + 1)
                    values(A, b, g, 0)
                    turn_probabilities(A, 1)
                    score(A, 2)
                    project_t(b, g, "q1", n + 1)
                    values(A, b, g, 1)
                    turn_probabilities(A, 2)
                    score(A, 3)
                    project_t(b, g, "k0", n + 2)
                    values(A, b, g, 2)
                    turn_probabilities(A, 3)
                    project_t(b, g, "k1", n + 2)
                    values(A, b, g, 3)
                    turn_output(A, b, g)
                    return
                cuts = (0, 4, 8) if kind == "inner" else (0, 2, 5, 8)
                project_out(b, g, "w", cuts[0], cuts[1], n + 1)
                values(A, b, g, 0)
                turn_probabilities(A, 1)
                score(A, 2)
                project_out(b, g, "w", cuts[1], cuts[2], n + 1)
                values(A, b, g, 1)
                turn_probabilities(A, 2)
                score(A, 3)
                if kind == "inner":
                    project_t(b, g, "q0", n + 2)
                else:
                    project_out(b, g, "w", cuts[2], cuts[3], n + 1)
                values(A, b, g, 2)
                turn_probabilities(A, 3)
                if kind == "inner":
                    project_t(b, g, "q1", n + 2)
                    values(A, b, g, 3)
                    project_t(b, g, "k0", n + 3)
                    turn_output(A, b, g)
                    project_t(b, g, "k1", n + 3)
                else:
                    values(A, b, g, 3)
                    turn_output(A, b, g)
                    wait_copied(pe, b, g, "t0")
                    wait_copied(pe, b, g, "t1")
                    project_out(b, g, "o", 0, 3, n + 2)
                    turn_h(b, 0)
                    for i in range(1, TILES):
                        project_out(b, g, "o", 2 * i + 1, min(2 * i + 3, 2 * TILES), n + 2)
                        logits(b, i - 1)
                        turn_h(b, i)
                    logits(b, TILES - 1)

            def turn_h(b, i):
                wait_copied(pe, b, GROUPS - 1, f"o{2 * i}")
                wait_copied(pe, b, GROUPS - 1, f"o{2 * i + 1}")
                if i >= 2:
                    pe.wait_ge(rt_act, TILES * b + i - 1)
                    pe.wait_ge(rt_dve, TILES * b + i - 1)
                for kc in range(KC):
                    last = nc.tensor.transpose(bank(ROUTER_BANKS[i % 2], 2)[:, kc * P:(kc + 1) * P], xh[:, i, kc * P:(kc + 1) * P], ident[:, :])
                last.then_inc(rt_mm, 1)

            def logits(b, i):
                pe.wait_ge(rw_done, 1)
                pe.wait_ge(rt_act, TILES * b + i + 1)
                pe.wait_ge(rt_dve, TILES * b + i + 1)
                for kc in range(KC):
                    last = nc.tensor.matmul(bank(4)[:, i * E:(i + 1) * E], rt[i % 2][:, kc * P:(kc + 1) * P], rw[:, kc, :],
                                            start=kc == 0, stop=kc == KC - 1)
                last.then_inc(rt_used, 1)

            def turn_x(b):
                pe.wait_ge(xe_done, TILES * (b + 1))
                for kc in range(KC):
                    if kc >= len(NORM_BANKS):
                        pe.wait_ge(utr_done, KC * b + kc - len(NORM_BANKS) + 1)
                    for i in range(TILES):
                        last = nc.tensor.transpose(bank(NORM_BANKS[kc % 4])[:, i * P:(i + 1) * P], early_t[:, i, kc * P:(kc + 1) * P], ident[:, :])
                    last.then_inc(xt_front, 1)

            def before_groups(b):
                n = len(PAIRS) * b
                for job, pair in (("q0", n), ("q1", n), ("k0", n + 1), ("k1", n + 1)):
                    project_t(b, None, job, pair)

            pe.wait_ge(const_in, 16 * 2)
            turn_x(0)
            before_groups(0)
            for b in range(TRUNKS):
                pe.wait_ge(zeros_done, 2 * (b + 1))
                if b:
                    pe.wait_ge(lg_step, 3 * b)
                group(b, 0)
                with pe.Fori(1, GROUPS - 1) as g:
                    group(b, g)
                group(b, GROUPS - 1)
                if b + 1 < TRUNKS:
                    turn_x(b + 1)
                    before_groups(b + 1)

            pe.wait_ge(aff_done, 3 * TRUNKS)
            for i in range(TILES):
                last = nc.tensor.transpose(bank(0)[0:TRUNKS * E, i * P:(i + 1) * P], aff[:, i, :], ident[:, :])
            last.then_inc(afft_mm, 1)
            pe.wait_ge(top_done, 4)
            for k, table in enumerate((gv, gi)):
                last = nc.tensor.transpose(bank(1)[:, k * 2 * E:(k + 1) * 2 * E], table[:, :, :].rearrange("e a s -> e (a s)"),
                                           ident[0:TRUNKS * E, 0:TRUNKS * E])
            last.then_inc(route_mm, 1)

            def rows_t(e, before):
                pe.wait_ge(gathered, 16 * (e + 1))
                if before is not None:
                    pe.wait_ge(htr_done, before)
                for kc in range(KC):
                    last = nc.tensor.transpose(bank(6, 2)[:, kc * P:(kc + 1) * P], xg[:, kc * P:(kc + 1) * P], ident[:, :])
                last.then_inc(xt_mm, 1)

            def gate_up(s, q_of):
                for i in range(GU_PAIRS):
                    j = i % SLOTS
                    pe.wait_ge(rest_done, SLOTS * q_of(i) + j + 1)
                    for k in range(2):
                        kc = 2 * (i // 2) + k
                        at = slice(kc * P, (kc + 1) * P)
                        last = products([(bank(2 * (i % 2) + n), xt_high[:, at], xt_rest[:, at], *w(j, k * HALF + n * BANK, BANK),
                                          kc == 0, kc == KC - 1) for n in range(2)])
                    last.then_inc(pair_used, 1)

            def down(s, h, q_of, lo, first=0, end=D_PAIRS, lhs=(ht_high, ht_rest)):
                pe.wait_ge(htr_done, s + 1)
                for i in range(lo + first, lo + end):
                    j = i % SLOTS
                    pe.wait_ge(rest_done, SLOTS * q_of(i) + j + 1)
                    for k in range(2):
                        c = 2 * (i - lo) + k
                        at = slice(c * P, (c + 1) * P)
                        last = products([(bank(4 + n), lhs[0][:, at], lhs[1][:, at], *w(j, k * D + n * BANK, BANK),
                                          h == 0 and c == 0, h == 1 and c == 7) for n in range(2)])
                    last.then_inc(pair_used, 1)

            def hidden_t(s):
                pe.wait_ge(hid_done, s + 1)
                for c in range(HALF // P):
                    last = nc.tensor.transpose(bank(6, 2)[:, c * P:(c + 1) * P], hid[:, c * P:(c + 1) * P], ident[:, :])
                last.then_inc(ht_mm, 1)

            rows_t(0, None)
            pe.wait_ge(xtr_done, 1)
            gate_up(0, lambda i: FRONT_Q + i // SLOTS)
            hidden_t(0)
            with pe.Fori(0, E - 1) as e:
                at = lambda s: lambda i: body_q(e, s + i)
                gate_up(2 * e + 1, at(0))
                rows_t(e + 1, 2 * e + 1)
                pe.wait_ge(ys_done, e + 1)
                down(2 * e, 0, at(0), 8)
                pe.wait_ge(xtr_done, e + 2)
                hidden_t(2 * e + 1)
                gate_up(2 * e + 2, at(12))
                down(2 * e + 1, 1, at(0), 20)
                hidden_t(2 * e + 2)
            at = lambda s: lambda i: body_q(E - 1, s + i)
            gate_up(2 * E - 1, at(0))
            pe.wait_ge(ys_done, E)
            down(2 * E - 2, 0, at(0), 8, 0, 2)
            hidden_t(2 * E - 1)
            down(2 * E - 2, 0, at(0), 8, 2, 4)
            down(2 * E - 1, 1, at(0), 12, lhs=(xt_high, xt_rest))
            pe.wait_ge(one_hot_done, 1)
            pe.wait_ge(ysr_done, 1)
            for t in range(TRUNKS * TILES):
                if t >= 3:
                    pe.wait_ge(h_done, t - 2)
                for part in (ys_high, ys_rest):
                    for n in range(2):
                        last = nc.tensor.matmul(bank(ADD_BANKS[t % 3] + n), one_hot[:, t * P:(t + 1) * P], part[:, n * BANK:(n + 1) * BANK],
                                                start=part is ys_high, stop=part is ys_rest)
                last.then_inc(add_mm, 1)


def bias_layout(rpb):
    q, k = np.arange(P), np.arange(WIN)
    out = []
    for i in (0, 1, 3):
        qc, kcol = QCOLS * i + q // ROWS, WIN_COL[i] + k // ROWS
        start = np.clip(qc - KW // 2, 0, GRID_W - KW)
        inside = (kcol[None] >= start[:, None]) & (kcol[None] < start[:, None] + KW)
        dr = (k % ROWS)[None] - (q % ROWS)[:, None] + KH - 1
        dc = np.where(inside, kcol[None] - qc[:, None] + KW - 1, 0)
        out.append(np.where(inside[None], rpb[:, dr, dc], np.float32(MASKED)))
    return np.ascontiguousarray(np.stack(out, 2).reshape(HEADS * P, 3 * WIN))


def kernel(x_prompt, x_sample, norm_mix_g, norm_ffn_g, final_norm_g, na_w_qkv, na_rpb, na_w_o, pool_w, pool_scale,
           gla_w_in, gla_w_gate_f, gla_b_gate_f, gla_w_gate_b, gla_b_gate_b, gla_norm_g, gla_w_o,
           router_w, moe_w_gate, moe_w_up, moe_w_down):
    import concourse.bacc as bacc
    from concourse.bass_utils import run_bass_kernel_spmd

    by_column = lambda a: np.asarray(a).reshape(ROWS, GRID_W, D).transpose(1, 0, 2).reshape(T, D)
    by_row = lambda a: np.ascontiguousarray(a.reshape(GRID_W, ROWS, D).transpose(1, 0, 2).reshape(1, T, D))
    arrays = {
        "x": np.concatenate([by_column(x_prompt), by_column(x_sample)]),
        "g_mix": np.ascontiguousarray(np.asarray(norm_mix_g).reshape(KC, P).T),
        "g_ffn_col": np.ascontiguousarray(np.asarray(norm_ffn_g).reshape(KC, P).T),
        "g_ffn": np.asarray(norm_ffn_g).reshape(1, D),
        "g_fin": np.asarray(final_norm_g).reshape(1, D),
        "w_qkv": np.asarray(na_w_qkv)[0],
        "bias": bias_layout(np.asarray(na_rpb)[0]),
        "w_o": np.asarray(na_w_o)[0],
        "router_w": np.asarray(router_w)[0],
        "w_gate": np.asarray(moe_w_gate).reshape(E * D, F),
        "w_up": np.asarray(moe_w_up).reshape(E * D, F),
        "w_down": np.asarray(moe_w_down).reshape(E * F, D),
        "identity": np.eye(P, dtype=np.float32),
        "token_numbers": np.arange(TRUNKS * T, dtype=np.float32).reshape(1, TRUNKS * T),
    }
    nc = bacc.Bacc("TRN2", target_bir_lowering=False, num_devices=1)
    args = {n: nc.dram_tensor(n, a.shape, mybir.dt.from_np(a.dtype), kind="ExternalInput").ap() for n, a in arrays.items()}
    y = nc.dram_tensor("y", (TRUNKS * T, D), F32, kind="ExternalOutput").ap()
    encoder_kernel(nc, *[args[n] for n in arrays], y)
    got = run_bass_kernel_spmd(nc, [arrays], core_ids=[0]).results[0]["y"]
    return by_row(got[:T]), by_row(got[T:])
```
